# Optimizing a Trainium2 kernel written in Bass

```python
import math
import jax, jax.numpy as jnp
from jax import lax
import numpy as np

D_MODEL = 1024
BATCH = 1
SEQ = 256
DEPTH = 4

N_MIXERS = 3
N_A_LAYERS = (DEPTH + 2) // 3
N_B_LAYERS = (DEPTH + 1) // 3
N_C_LAYERS = DEPTH // 3

RMS_EPS = 1e-6
CONV_W = 3

NA_HEAD_DIM = 64
NA_HEADS = D_MODEL // NA_HEAD_DIM
GRID_W = 64
NA_MAX_ROWS = 8
NA_COLS = 16
NA_QCOLS = 16
NA_SPAN = NA_QCOLS + NA_COLS

HYENA_ORDER = 2
HYENA_BANDS = 16
HYENA_EMB = 1 + 2 * HYENA_BANDS
HYENA_FILTER_HIDDEN = 64
HYENA_DECAY_TARGET = 1e-2
HYENA_FAST_DECAY = 0.3
HYENA_SLOW_DECAY = 1.5

FFN_HIDDEN = ((8 * D_MODEL + 3 * 256 - 1) // (3 * 256)) * 256


def rmsnorm(x, g):
    xf = x.astype(jnp.float32)
    y = xf * lax.rsqrt(jnp.mean(xf * xf, axis=-1, keepdims=True) + RMS_EPS)
    return (y * g.astype(jnp.float32)).astype(x.dtype)

def depthwise_conv3(x, w, b=None):
    c = x.shape[-1]
    y = lax.conv_general_dilated(
        x, w.astype(x.dtype)[:, None, :], (1,), ((CONV_W // 2, CONV_W // 2),),
        dimension_numbers=('NWC', 'WIO', 'NWC'), feature_group_count=c)
    return y if b is None else y + b.astype(x.dtype)

def short_conv_mixer(h, w_in, conv_w, w_out):
    b_gate, c_gate, u = jnp.split(h @ w_in, 3, axis=-1)
    return (b_gate * depthwise_conv3(c_gate * u, conv_w)) @ w_out

def na_column_tables():
    cb = np.arange(GRID_W // NA_QCOLS)
    starts = np.clip(cb * NA_QCOLS - NA_COLS // 2, 0, GRID_W - NA_SPAN)
    key_col = starts[:, None] + np.arange(NA_SPAN)
    q_col = cb[:, None] * NA_QCOLS + np.arange(NA_QCOLS)
    col_start = np.clip(q_col - NA_COLS // 2, 0, GRID_W - NA_COLS)
    kc = key_col[:, None, :]
    valid = (kc >= col_start[:, :, None]) & (kc < col_start[:, :, None] + NA_COLS)
    dc_idx = np.clip(kc - q_col[:, :, None] + NA_COLS - 1, 0, 2 * NA_COLS - 2)
    return key_col, valid, dc_idx

def neighborhood_attention(h, w_qkv, q_g, k_g, rpb, w_out):
    bsz, seq, d = h.shape
    rows = seq // GRID_W
    wr = min(NA_MAX_ROWS, rows)
    q, k, v = jnp.split(h @ w_qkv, 3, axis=-1)
    grid = (bsz, rows, GRID_W, NA_HEADS, NA_HEAD_DIM)
    q = rmsnorm(q.reshape(grid), q_g)
    k = rmsnorm(k.reshape(grid), k_g)
    v = v.reshape(grid)
    key_col, valid, dc_idx = na_column_tables()
    ncb = key_col.shape[0]
    scale = NA_HEAD_DIM ** -0.5
    neg = jnp.finfo(jnp.float32).min
    mask = valid[None, None, :, :, None, :]

    def row_block(r):
        rs = jnp.clip(r - wr // 2, 0, rows - wr)
        q_r = lax.dynamic_index_in_dim(q, r, axis=1, keepdims=False)
        q_r = q_r.reshape(bsz, ncb, NA_QCOLS, NA_HEADS, NA_HEAD_DIM)
        k_r = lax.dynamic_slice_in_dim(k, rs, wr, axis=1)[:, :, key_col]
        v_r = lax.dynamic_slice_in_dim(v, rs, wr, axis=1)[:, :, key_col]
        s = jnp.einsum('bnqhd,brnkhd->bhnqrk', q_r, k_r).astype(jnp.float32) * scale
        dr_idx = rs + jnp.arange(wr) - r + NA_MAX_ROWS - 1
        bias = rpb[:, dr_idx[None, None, :, None], dc_idx[:, :, None, :]]
        s = jnp.where(mask, s + bias.astype(jnp.float32)[None], neg)
        p = jax.nn.softmax(s.reshape(s.shape[:4] + (wr * NA_SPAN,)), axis=-1)
        p = p.reshape(s.shape).astype(v.dtype)
        o = jnp.einsum('bhnqrk,brnkhd->bnqhd', p, v_r)
        return o.reshape(bsz, GRID_W, d)

    o = lax.map(row_block, jnp.arange(rows))
    return o.transpose(1, 0, 2, 3).reshape(bsz, seq, d) @ w_out

def hyena_filters(seq, w1, b1, w2, b2, w3, freq):
    f32 = jnp.float32
    t = jnp.linspace(0.0, 1.0, seq, dtype=f32)[:, None]
    bands = jnp.linspace(1e-4, HYENA_BANDS - 1, HYENA_BANDS, dtype=f32)
    ang = (2.0 * math.pi) * jnp.arange(seq, dtype=f32)[:, None] / seq * bands
    z = jnp.concatenate([t, jnp.cos(ang), -jnp.sin(ang)], axis=-1)
    fr = freq.astype(f32)
    hid = jnp.sin(fr * (z @ w1.astype(f32) + b1.astype(f32)))
    hid = jnp.sin(fr * (hid @ w2.astype(f32) + b2.astype(f32)))
    filt = (hid @ w3.astype(f32)).reshape(seq, HYENA_ORDER, 2, D_MODEL)
    lt = math.log(HYENA_DECAY_TARGET)
    deltas = jnp.abs(jnp.linspace(lt / HYENA_SLOW_DECAY, lt / HYENA_FAST_DECAY, D_MODEL, dtype=f32))
    filt = filt * jnp.exp(-t * deltas)[:, None, None, :]
    fwd, rev = filt[:, :, 0], filt[:, :, 1]
    h_full = jnp.concatenate([fwd[:1] + rev[:1], fwd[1:], jnp.zeros_like(fwd[:1]), rev[:0:-1]], axis=0)
    h_full = h_full / jnp.sum(jnp.abs(h_full), axis=0, keepdims=True)
    return jnp.fft.rfft(h_full, axis=0)

def hyena_mixer(h, w_in, short_w, short_b, f_w1, f_b1, f_w2, f_b2, f_w3, f_freq, f_skip, w_out):
    seq = h.shape[1]
    v, x1, x2 = jnp.split(depthwise_conv3(h @ w_in, short_w, short_b), 3, axis=-1)
    h_freq = hyena_filters(seq, f_w1, f_b1, f_w2, f_b2, f_w3, f_freq)

    def long_conv(u, n):
        uf = u.astype(jnp.float32)
        y = jnp.fft.irfft(jnp.fft.rfft(uf, n=2 * seq, axis=1) * h_freq[:, n], n=2 * seq, axis=1)[:, :seq]
        return (y + uf * f_skip[n].astype(jnp.float32)).astype(u.dtype)

    z = x1 * long_conv(v, 0)
    z = x2 * long_conv(z, 1)
    return z @ w_out

def swiglu(h, w13, w2):
    g, u = jnp.split(h @ w13, 2, axis=-1)
    return (jax.nn.silu(g) * u) @ w2

def first_inputs(seed: int = 0) -> dict:
    key = jax.random.key(seed)
    ks = jax.random.split(key, 24)
    f32 = jnp.float32

    def nrm(k, shape, fan_in):
        return jax.random.normal(k, shape, f32) * (fan_in ** -0.5)

    def gain(k, shape):
        return 1.0 + 0.02 * jax.random.normal(k, shape, f32)

    def small(k, shape, s=0.02):
        return s * jax.random.normal(k, shape, f32)

    D = D_MODEL
    return {
        'x': jax.random.normal(ks[0], (BATCH, SEQ, D), f32),
        'norm_mix_g': gain(ks[1], (DEPTH, D)),
        'norm_ffn_g': gain(ks[2], (DEPTH, D)),
        'a_w_in': nrm(ks[3], (N_A_LAYERS, D, 3 * D), D),
        'a_conv_w': nrm(ks[4], (N_A_LAYERS, CONV_W, D), CONV_W),
        'a_w_out': nrm(ks[5], (N_A_LAYERS, D, D), D),
        'b_w_qkv': nrm(ks[6], (N_B_LAYERS, D, 3 * D), D),
        'b_q_norm_g': gain(ks[7], (N_B_LAYERS, NA_HEAD_DIM)),
        'b_k_norm_g': gain(ks[8], (N_B_LAYERS, NA_HEAD_DIM)),
        'b_rpb': small(ks[9], (N_B_LAYERS, NA_HEADS, 2 * NA_MAX_ROWS - 1, 2 * NA_COLS - 1)),
        'b_w_out': nrm(ks[10], (N_B_LAYERS, D, D), D),
        'c_w_in': nrm(ks[11], (N_C_LAYERS, D, 3 * D), D),
        'c_short_w': nrm(ks[12], (N_C_LAYERS, CONV_W, 3 * D), CONV_W),
        'c_short_b': small(ks[13], (N_C_LAYERS, 3 * D)),
        'c_f_w1': nrm(ks[14], (N_C_LAYERS, HYENA_EMB, HYENA_FILTER_HIDDEN), HYENA_EMB),
        'c_f_b1': small(ks[15], (N_C_LAYERS, HYENA_FILTER_HIDDEN)),
        'c_f_w2': nrm(ks[16], (N_C_LAYERS, HYENA_FILTER_HIDDEN, HYENA_FILTER_HIDDEN), HYENA_FILTER_HIDDEN),
        'c_f_b2': small(ks[17], (N_C_LAYERS, HYENA_FILTER_HIDDEN)),
        'c_f_w3': nrm(ks[18], (N_C_LAYERS, HYENA_FILTER_HIDDEN, HYENA_ORDER * 2 * D), HYENA_FILTER_HIDDEN),
        'c_f_freq': gain(ks[19], (N_C_LAYERS, HYENA_FILTER_HIDDEN)),
        'c_f_skip': small(ks[20], (N_C_LAYERS, HYENA_ORDER, D), 0.5),
        'c_w_out': nrm(ks[21], (N_C_LAYERS, D, D), D),
        'f_w13': nrm(ks[22], (DEPTH, D, 2 * FFN_HIDDEN), D),
        'f_w2': nrm(ks[23], (DEPTH, FFN_HIDDEN, D), FFN_HIDDEN),
    }

def first_block(x, norm_mix_g, norm_ffn_g, a_w_in, a_conv_w, a_w_out,
              b_w_qkv, b_q_norm_g, b_k_norm_g, b_rpb, b_w_out,
              c_w_in, c_short_w, c_short_b, c_f_w1, c_f_b1, c_f_w2, c_f_b2,
              c_f_w3, c_f_freq, c_f_skip, c_w_out, f_w13, f_w2):
    ia = ib = ic = 0
    for i in range(DEPTH):
        h = rmsnorm(x, norm_mix_g[i])
        kind = i % N_MIXERS
        if kind == 0:
            y = short_conv_mixer(h, a_w_in[ia], a_conv_w[ia], a_w_out[ia])
            ia += 1
        elif kind == 1:
            y = neighborhood_attention(h, b_w_qkv[ib], b_q_norm_g[ib], b_k_norm_g[ib], b_rpb[ib], b_w_out[ib])
            ib += 1
        else:
            y = hyena_mixer(h, c_w_in[ic], c_short_w[ic], c_short_b[ic], c_f_w1[ic], c_f_b1[ic],
                            c_f_w2[ic], c_f_b2[ic], c_f_w3[ic], c_f_freq[ic], c_f_skip[ic], c_w_out[ic])
            ic += 1
        x = x + y
        x = x + swiglu(rmsnorm(x, norm_ffn_g[i]), f_w13[i], f_w2[i])
    return x


DEPTH_2 = 1

N_META = 16
CHUNK = 128
META_PAD = (-N_META) % CHUNK
RET_HEADS = 8
RET_DK = 64
RET_DV = 128
RET_QK_W = RET_HEADS * RET_DK
RET_V_W = RET_HEADS * RET_DV
MLA_HEADS = 8
MLA_Q_RANK = 384
MLA_KV_RANK = 256
MLA_NOPE = 64
MLA_ROPE = 32
MLA_DV = 64
MLA_QK = MLA_NOPE + MLA_ROPE
D_FF = ((-(-8 * D_MODEL // 3) + 255) // 256) * 256
ROPE_BASE = 10000.0
GN_EPS = 1e-5

SPLIT_SIZES = (RET_QK_W, RET_QK_W, RET_V_W, RET_V_W, MLA_Q_RANK, MLA_KV_RANK, MLA_ROPE, D_MODEL, D_MODEL)
SPLIT_IDX = tuple(int(s) for s in np.cumsum(SPLIT_SIZES)[:-1])
D_IN = int(sum(SPLIT_SIZES))


def _rmsnorm(x, w):
    xf = x.astype(jnp.float32)
    y = xf * lax.rsqrt(jnp.mean(xf * xf, axis=-1, keepdims=True) + RMS_EPS)
    return (y * w.astype(jnp.float32)).astype(x.dtype)

def _rope_tables(pos, dim):
    half = dim // 2
    inv = ROPE_BASE ** (-jnp.arange(half, dtype=jnp.float32) / half)
    ang = pos.astype(jnp.float32)[:, None] * inv[None, :]
    return jnp.cos(ang), jnp.sin(ang)

def _apply_rope(x, cos, sin):
    half = x.shape[-1] // 2
    xf = x.astype(jnp.float32)
    x1, x2 = xf[..., :half], xf[..., half:]
    return jnp.concatenate([x1 * cos - x2 * sin, x1 * sin + x2 * cos], axis=-1).astype(x.dtype)

def _retention_dir(q, k, v, log_gamma, inclusive):
    B, Lp, H, dk = q.shape
    dv = v.shape[-1]
    n = Lp // CHUNK
    qc = q.reshape(B, n, CHUNK, H, dk)
    kc = k.reshape(B, n, CHUNK, H, dk)
    vc = v.reshape(B, n, CHUNK, H, dv)
    lg = log_gamma.astype(jnp.float32)
    idx = jnp.arange(CHUNK, dtype=jnp.float32)
    rel = idx[:, None] - idx[None, :]
    mask = rel >= 0 if inclusive else rel > 0
    dmask = jnp.exp(jnp.where(mask[None], lg[:, None, None] * rel[None], -jnp.inf)).astype(q.dtype)
    scores = jnp.einsum('bnihd,bnjhd->bnhij', qc, kc) * dmask
    inner = jnp.einsum('bnhij,bnjhe->bnihe', scores, vc)
    w_k = jnp.exp(lg[None, :] * (CHUNK - 1 - idx)[:, None]).astype(q.dtype)
    incr = jnp.einsum('bnjhd,jh,bnjhe->nbhde', kc, w_k, vc)
    g_chunk = jnp.exp(lg * CHUNK).astype(incr.dtype)[None, :, None, None]

    def step(state, u):
        return g_chunk * state + u, state

    state0 = jnp.zeros((B, H, dk, dv), incr.dtype)
    _, states_prev = lax.scan(step, state0, incr)
    w_q = jnp.exp(lg[None, :] * (idx + 1.0)[:, None]).astype(q.dtype)
    cross = jnp.einsum('bnihd,ih,nbhde->bnihe', qc, w_q, states_prev)
    return (inner + cross).reshape(B, Lp, H, dv)

def _bidir_retention(q, k, v, decay_f, decay_b):
    lg_f = -jnp.exp(decay_f.astype(jnp.float32))
    lg_b = -jnp.exp(decay_b.astype(jnp.float32))
    pad = ((0, 0), (META_PAD, 0), (0, 0), (0, 0))
    qp, kp, vp = jnp.pad(q, pad), jnp.pad(k, pad), jnp.pad(v, pad)
    fwd = _retention_dir(qp, kp, vp, lg_f, True)
    bwd = jnp.flip(_retention_dir(jnp.flip(qp, 1), jnp.flip(kp, 1), jnp.flip(vp, 1), lg_b, False), 1)
    return (fwd + bwd)[:, META_PAD:]

def _head_group_norm(y, w):
    B, L, H, dv = y.shape
    yf = y.astype(jnp.float32)
    mu = jnp.mean(yf, axis=-1, keepdims=True)
    var = jnp.mean(jnp.square(yf - mu), axis=-1, keepdims=True)
    yn = ((yf - mu) * lax.rsqrt(var + GN_EPS)).reshape(B, L, H * dv)
    return (yn * w.astype(jnp.float32)).astype(y.dtype)

def _mla_attention(q_nope, q_rope, k_nope, k_rope, v):
    B, L, H, _ = q_nope.shape
    Lp = L + META_PAD
    nb = Lp // CHUNK
    scale = MLA_QK ** -0.5

    def to_blocks(t):
        t = jnp.pad(t, ((0, 0), (META_PAD, 0), (0, 0), (0, 0)))
        return t.reshape(B, nb, CHUNK, H, t.shape[-1]).swapaxes(0, 1)

    def attend(qb):
        qn, qr = qb
        s = jnp.einsum('bqhd,bkhd->bhqk', qn, k_nope) + jnp.einsum('bqhr,bkr->bhqk', qr, k_rope)
        p = jax.nn.softmax(s.astype(jnp.float32) * scale, axis=-1).astype(v.dtype)
        return jnp.einsum('bhqk,bkhd->bqhd', p, v)

    out = lax.map(attend, (to_blocks(q_nope), to_blocks(q_rope)))
    return out.swapaxes(0, 1).reshape(B, Lp, H, MLA_DV)[:, META_PAD:]

def _mixer(u, w_in, decay_f, decay_b, gn_w, w_ret_out, q_norm_w, w_uq, kv_norm_w, w_uk, w_uv,
           w_mla_out, w_o, ret_cos, ret_sin, mla_cos, mla_sin):
    B, L, _ = u.shape
    proj = u @ w_in
    rq, rk, rv, rg, a_cq, a_ckv, a_kr, a_gret, a_gmla = jnp.split(proj, SPLIT_IDX, axis=-1)

    rq = _apply_rope(rq.reshape(B, L, RET_HEADS, RET_DK), ret_cos[:, None, :], ret_sin[:, None, :])
    rk = _apply_rope(rk.reshape(B, L, RET_HEADS, RET_DK), ret_cos[:, None, :], ret_sin[:, None, :]) * (RET_DK ** -0.5)
    rv = rv.reshape(B, L, RET_HEADS, RET_DV)
    y_ret = _head_group_norm(_bidir_retention(rq, rk, rv, decay_f, decay_b), gn_w)
    y_ret = (jax.nn.silu(rg) * y_ret) @ w_ret_out

    c_q = _rmsnorm(a_cq, q_norm_w)
    q = (c_q @ w_uq).reshape(B, L, MLA_HEADS, MLA_QK)
    q_nope = q[..., :MLA_NOPE]
    q_rope = _apply_rope(q[..., MLA_NOPE:], mla_cos[:, None, :], mla_sin[:, None, :])
    c_kv = _rmsnorm(a_ckv, kv_norm_w)
    k_nope = (c_kv @ w_uk).reshape(B, L, MLA_HEADS, MLA_NOPE)
    v = (c_kv @ w_uv).reshape(B, L, MLA_HEADS, MLA_DV)
    k_rope = _apply_rope(a_kr, mla_cos, mla_sin)
    y_mla = _mla_attention(q_nope, q_rope, k_nope, k_rope, v).reshape(B, L, MLA_HEADS * MLA_DV) @ w_mla_out

    merged = jax.nn.sigmoid(a_gret) * y_ret + jax.nn.sigmoid(a_gmla) * y_mla
    return merged @ w_o

def _swiglu(u, w_gate, w_up, w_down):
    return (jax.nn.silu(u @ w_gate) * (u @ w_up)) @ w_down

def second_inputs(seed: int = 0) -> dict:
    key = jax.random.key(seed)
    ks = jax.random.split(key, 24)
    f32 = jnp.float32

    def nrm(k, shape, fan_in):
        return jax.random.normal(k, shape, f32) * (fan_in ** -0.5)

    def gain(k, shape):
        return 1.0 + 0.02 * jax.random.normal(k, shape, f32)

    h_idx = jnp.arange(RET_HEADS, dtype=f32)
    gamma = 1.0 - 2.0 ** (-5.0 - h_idx)
    decay_base = jnp.log(-jnp.log(gamma))
    return {
        'x': jax.random.normal(ks[0], (BATCH, SEQ, D_MODEL), f32),
        'meta_tokens': jax.random.normal(ks[1], (N_META, D_MODEL), f32),
        'norm_mix_w': gain(ks[2], (DEPTH_2, D_MODEL)),
        'w_in': nrm(ks[3], (DEPTH_2, D_MODEL, D_IN), D_MODEL),
        'ret_decay_fwd': decay_base[None] + 0.05 * jax.random.normal(ks[4], (DEPTH_2, RET_HEADS), f32),
        'ret_decay_bwd': decay_base[None] + 0.05 * jax.random.normal(ks[5], (DEPTH_2, RET_HEADS), f32),
        'ret_gn_w': gain(ks[6], (DEPTH_2, RET_V_W)),
        'w_ret_out': nrm(ks[7], (DEPTH_2, RET_V_W, D_MODEL), RET_V_W),
        'mla_q_norm_w': gain(ks[8], (DEPTH_2, MLA_Q_RANK)),
        'w_uq': nrm(ks[9], (DEPTH_2, MLA_Q_RANK, MLA_HEADS * MLA_QK), MLA_Q_RANK),
        'mla_kv_norm_w': gain(ks[10], (DEPTH_2, MLA_KV_RANK)),
        'w_uk': nrm(ks[11], (DEPTH_2, MLA_KV_RANK, MLA_HEADS * MLA_NOPE), MLA_KV_RANK),
        'w_uv': nrm(ks[12], (DEPTH_2, MLA_KV_RANK, MLA_HEADS * MLA_DV), MLA_KV_RANK),
        'w_mla_out': nrm(ks[13], (DEPTH_2, MLA_HEADS * MLA_DV, D_MODEL), MLA_HEADS * MLA_DV),
        'w_o': nrm(ks[14], (DEPTH_2, D_MODEL, D_MODEL), D_MODEL),
        'norm_ffn_w': gain(ks[15], (DEPTH_2, D_MODEL)),
        'w_ffn_gate': nrm(ks[16], (DEPTH_2, D_MODEL, D_FF), D_MODEL),
        'w_ffn_up': nrm(ks[17], (DEPTH_2, D_MODEL, D_FF), D_MODEL),
        'w_ffn_down': nrm(ks[18], (DEPTH_2, D_FF, D_MODEL), D_FF),
        'norm_final_w': gain(ks[19], (D_MODEL,)),
    }

def second_block(x, meta_tokens, norm_mix_w, w_in, ret_decay_fwd, ret_decay_bwd, ret_gn_w, w_ret_out,
              mla_q_norm_w, w_uq, mla_kv_norm_w, w_uk, w_uv, w_mla_out, w_o, norm_ffn_w,
              w_ffn_gate, w_ffn_up, w_ffn_down, norm_final_w):
    B, S, D = x.shape
    L = S + N_META
    meta = jnp.broadcast_to(meta_tokens.astype(x.dtype)[None], (B, N_META, D))
    h = jnp.concatenate([meta, x], axis=1)
    pos = jnp.arange(L)
    ret_cos, ret_sin = _rope_tables(pos, RET_DK)
    mla_cos, mla_sin = _rope_tables(pos, MLA_ROPE)
    for l in range(DEPTH_2):
        h = h + _mixer(_rmsnorm(h, norm_mix_w[l]), w_in[l], ret_decay_fwd[l], ret_decay_bwd[l], ret_gn_w[l],
                       w_ret_out[l], mla_q_norm_w[l], w_uq[l], mla_kv_norm_w[l], w_uk[l], w_uv[l],
                       w_mla_out[l], w_o[l], ret_cos, ret_sin, mla_cos, mla_sin)
        h = h + _swiglu(_rmsnorm(h, norm_ffn_w[l]), w_ffn_gate[l], w_ffn_up[l], w_ffn_down[l])
    h = _rmsnorm(h, norm_final_w)
    return h[:, N_META:]


def setup_inputs(seed=0):
    out = dict(first_inputs(seed))
    for name, value in second_inputs(seed + 1).items():
        if name != "x":
            out[name + "_2"] = value
    return out


def reference(
    x, norm_mix_g, norm_ffn_g, a_w_in, a_conv_w, a_w_out, b_w_qkv, b_q_norm_g, b_k_norm_g,
    b_rpb, b_w_out, c_w_in, c_short_w, c_short_b, c_f_w1, c_f_b1, c_f_w2, c_f_b2, c_f_w3,
    c_f_freq, c_f_skip, c_w_out, f_w13, f_w2, meta_tokens_2, norm_mix_w_2, w_in_2,
    ret_decay_fwd_2, ret_decay_bwd_2, ret_gn_w_2, w_ret_out_2, mla_q_norm_w_2, w_uq_2,
    mla_kv_norm_w_2, w_uk_2, w_uv_2, w_mla_out_2, w_o_2, norm_ffn_w_2, w_ffn_gate_2, w_ffn_up_2,
    w_ffn_down_2, norm_final_w_2,
):
    x = first_block(
        x, norm_mix_g, norm_ffn_g, a_w_in, a_conv_w, a_w_out, b_w_qkv, b_q_norm_g, b_k_norm_g,
        b_rpb, b_w_out, c_w_in, c_short_w, c_short_b, c_f_w1, c_f_b1, c_f_w2, c_f_b2, c_f_w3,
        c_f_freq, c_f_skip, c_w_out, f_w13, f_w2,
    )
    return second_block(
        x, meta_tokens_2, norm_mix_w_2, w_in_2, ret_decay_fwd_2, ret_decay_bwd_2, ret_gn_w_2,
        w_ret_out_2, mla_q_norm_w_2, w_uq_2, mla_kv_norm_w_2, w_uk_2, w_uv_2, w_mla_out_2,
        w_o_2, norm_ffn_w_2, w_ffn_gate_2, w_ffn_up_2, w_ffn_down_2, norm_final_w_2,
    )


_drawn_inputs = setup_inputs


def setup_inputs(seed=0):
    import zlib

    import numpy as np

    out = dict(_drawn_inputs(seed))
    spreads = {}
    factors = {'b_q_norm_g': 8.0,
     'b_k_norm_g': 8.0,
     'b_rpb': 8.0,
     'c_short_b': 7.004,
     'c_f_b1': 8.0,
     'c_f_b2': 8.0,
     'c_f_freq': 8.0,
     'norm_mix_w_2': 8.0,
     'ret_gn_w_2': 8.0,
     'mla_q_norm_w_2': 8.0,
     'mla_kv_norm_w_2': 8.0,
     'norm_ffn_w_2': 7.53}
    for name, (base, spread) in spreads.items():
        noise = np.random.default_rng([zlib.crc32(name.encode()), seed]).standard_normal(out[name].shape)
        drawn = base * np.exp(spread * noise) if base else spread * noise
        out[name] = __import__('jax').numpy.asarray(drawn.astype(out[name].dtype))
    for name, factor in factors.items():
        out[name] = (out[name] * factor).astype(out[name].dtype)
    return out
```

```python
import math
from contextlib import ExitStack

import numpy as np
import concourse.bass as bass
from concourse import mybir

F32 = mybir.dt.float32
F32R = mybir.dt.float32r
ALU = mybir.AluOpType
ACT = mybir.ActivationFunctionType
AXX = mybir.AxisListType.X

P = 128
D = 1024
C = D // P
SEQ, META = 256, 16
L = SEQ + META
FF = 2816
FC = FF // P
DEPTH = 4
K8, K11 = 8, FC // 2
RING = 4
SLOT = K11 * P
EPS = 1e-6
GN_EPS = 1e-5
KINDS = ("conv", "attention", "hyena", "conv")

NH, HD, GW, GR = 16, 64, 64, 4
RH, RDK, RDV = 8, 64, 128
MH, NOPE, ROPE, MDV = 8, 64, 32, 64
MQK = NOPE + ROPE
QR, KR = 384, 256
JT = [(0, 128), (128, 128), (256, 16)]

EMB, FHID, NFFT = 33, 64, 2 * SEQ

VEC = {}


def _vec_layout():
    at = 0
    for name, n in (("mix_g", DEPTH * C), ("ffn_g", DEPTH * C), ("a_conv", 2 * 3 * C), ("c_conv", 3 * 24),
                    ("c_bias", 24), ("c_skip", 2 * C), ("mix_w2", C), ("ffn_w2", C), ("final_w", C), ("gn_w", C),
                    ("q_norm", QR // P), ("kv_norm", KR // P), ("q_g", 1), ("k_g", 1), ("f_b1", 1), ("f_b2", 1),
                    ("f_freq", 1)):
        VEC[name] = at
        at += n
    return at


NVEC = _vec_layout()

CON = {}


def _con_layout():
    at = 0
    for name, n in (("ident", P), ("ones", P), ("pair_ones", P), ("colmask", GW)):
        CON[name] = at
        at += n
    return at


NCON = _con_layout()


class Phase:

    def __init__(self, name, panels, k, panel0, tile0, bank0, tiles, block0):
        self.name, self.n, self.k, self.p0, self.t0, self.b0 = name, panels, k, panel0, tile0, bank0
        self.tiles, self.block0 = tiles, block0


def plan():
    out, p, t, b, at = {}, 0, 0, 0, {K8: 0, K11: 0}
    seq = []
    for layer in range(DEPTH):
        seq += [(f"in{layer}", 24, K8, 24), (f"out{layer}", 8, K8, 8), (f"up{layer}", 2 * FC, K8, 2 * FC),
                (f"down{layer}", 16, K11, 8)]
    seq += [("in_ret", 24, K8, 24), ("in_mla", 6, K8, 6), ("in_gate", 16, K8, 16), ("ret_out", 8, K8, 8),
            ("mla_out", 4, K8, 8), ("w_o", 8, K8, 8), ("up4", 2 * FC, K8, 2 * FC), ("down4", 16, K11, 8)]
    for name, n, k, tiles in seq:
        out[name] = Phase(name, n, k, p, t, b, tiles, at[k])
        p, t, at[k] = p + n, t + tiles, at[k] + n
        b = (b + (2 if k == K11 else tiles)) % 4
    names = [s[0] for s in seq]
    for a, nxt in zip(names, names[1:] + [None]):
        out[a].next_k = out[nxt].k if nxt else None
    return out, names, p


PH, ORDER, PANELS = plan()


RTAB = {"center": 0, "rot": P, "cos": 2 * P, "sin": 2 * P + L, "back": 2 * P + 2 * L, "ahead": 2 * P + 5 * L}
NRTAB = 2 * P + 8 * L
MTAB = {"rot": 0, "cos": P, "sin": P + L}
NMTAB = P + 2 * L

HC = 512
HJ = HC // P
YBASE = {"in0": 0, "in1": 8, "in2": 16, "in3": 24, "ret": 32, "mla": 40, "mrg": 44}
YR = {"in0": 0, "in3": C, "ret": 2 * C, "mrg": 3 * C}
NORMS = 2 * DEPTH + 3
TWO_PI_HI = 6.28125
TWO_PI_LO = 2 * math.pi - TWO_PI_HI
ROUND = 1.5 * 2.0 ** 23
PI_IN = 3.1415925


class Chain:

    def __init__(self, eng, sem):
        self.eng, self.sem, self.n = eng, sem, 0

    def __call__(self, ins):
        self.n = self.n + 1
        ins.then_inc(self.sem, 1)
        self.eng.wait_ge(self.sem, self.n)


def build(nc, a, out):
    ctx = ExitStack()

    def sem(name):
        return ctx.enter_context(nc.semaphore(name))

    def sb(name, shape, dt=F32):
        return ctx.enter_context(nc.sbuf_tensor(name, shape, dt))

    def overlay(scope, parts):
        got = {}
        with ExitStack() as stage:
            for name, shape, dt in parts:
                got[name] = stage.enter_context(nc.sbuf_tensor(f"{scope}_{name}", shape, dt))
        return got

    raw = sb("raw", [P, RING, SLOT])
    whi = sb("whi", [P, RING, SLOT], F32R)
    wlo = sb("wlo", [P, RING, SLOT], F32R)
    x = sb("x", [P, C, L])
    hyx = overlay("hyx", [("ab", [P, 2, 2, HC], F32), ("ut", [P, 2, HC], F32), ("am", [P, 2, HC], F32)])
    xh = sb("xh", [P, C, L], F32R)
    xl = sb("xl", [P, C, L], F32R)
    vec = sb("vec", [P, NVEC])
    con = sb("con", [P, NCON])
    eps = sb("eps", [P, 2])
    sumsq = sb("sumsq", [P, L])
    square = sb("square", [P, L])
    root = sb("root", [P, L])
    rinv = sb("rinv", [P, L])
    mean_sq = sb("mean_sq", [P, L])
    newton = sb("newton", [P, L])
    gate = sb("gate", [P, 2, L])
    silu = sb("silu", [P, 2, L])
    up = sb("up", [P, 2, L])
    hid = sb("hid", [P, 2, L])
    filt_hid = sb("filt_hid", [FHID, SEQ])
    bank = [ctx.enter_context(nc.psum_tensor(f"bank{i}", [P, 512], F32)) for i in range(8)]

    start = overlay("start", [("conv", [P, 40 * 256], F32), ("filt_in", [EMB, SEQ + FHID], F32),
                              ("filt_w2", [FHID, FHID], F32), ("filt_x", [FHID, SEQ], F32)])
    filt_in, filt_w2, filt_x = start["filt_in"], start["filt_w2"], start["filt_x"]
    ffn = overlay("ffn", [("hh", [P, FC, L], F32R), ("hl", [P, FC, L], F32R)])
    Y = [("yh", [P, C, L], F32R), ("yl", [P, C, L], F32R)]
    cm = overlay("conv", Y + [("c", [P, C, SEQ], F32), ("cv", [P, C, SEQ], F32), ("cu", [P, 2, SEQ + 2], F32)])
    att_fixed = [("qkv", [P, 24, SEQ], F32), ("bias", [P, NH, 6, GW], F32), ("nw", [P, 4, SEQ], F32),
                 ("sq", [P, 2, SEQ], F32)]
    at = overlay("att", Y + att_fixed + [("s", [P, 3, 2, SEQ], F32), ("pt", [P, 2, 2, SEQ], F32),
                                         ("vt", [P, 2, 2, P], F32), ("mx", [P, 3, 2], F32), ("sm", [P, 3, 2], F32),
                                         ("rs", [P, 3, 2], F32)])
    an = overlay("att_norm", [("ms", [P, 16, SEQ], F32), ("gap", [P, 2 * C * L - 16 * SEQ], F32)] +
                 att_fixed + [("rr", [P, 16, SEQ], F32)])
    hy = overlay("hy", Y + [("z", [P, 24, SEQ], F32), ("rawz", [P, 2, SEQ + 2], F32),
                            ("H", [P, 5, HC], F32), ("frY", [P, 4, HC], F32), ("t1", [P, HC], F32),
                            ("fdft", [P, 2, 2 * SEQ + P], F32), ("idft", [P, 4, SEQ], F32),
                            ("decay", [P, 2, HC], F32), ("w3", [FHID, 2, HC], F32), ("inv", [P, HJ], F32)]) | hyx
    rt = overlay("ret", Y + [("t", [P, 24, L], F32), ("vt", [P, 3, D], F32), ("e1", [P, 2, 3, L], F32),
                             ("e2", [P, 3, L], F32), ("sd", [P, 2, 3, L], F32), ("y", [P, L], F32),
                             ("sq", [P, L], F32), ("rr", [P, L], F32), ("tab", [P, NRTAB], F32),
                             ("dec", [P, 2, RH], F32), ("lg", [P, 2, RH], F32)])
    ML0 = [("retyh", [P, C, L], F32R), ("retyl", [P, C, L], F32R), ("yh", [P, 4, L], F32R), ("yl", [P, 4, L], F32R)]
    ml = overlay("mla", ML0 + [("c", [P, 6, L], F32), ("uq", [P, 3, MH * MQK], F32),
                               ("uk", [P, 2, MH * NOPE], F32), ("uv", [P, 2, MH * MDV], F32), ("q", [P, 2, L], F32),
                               ("qraw", [P, L], F32), ("k", [P, 2, L], F32), ("kr", [P, L], F32),
                               ("vt", [P, 3, MH * MDV], F32), ("sq", [P, 3, L], F32), ("rr", [P, 2, L], F32), ("ms", [P, L], F32), ("nw", [P, L], F32),
                               ("s", [P, 2, 3, L], F32), ("pt", [P, 3, L], F32), ("mx", [P, 2, 3], F32),
                               ("sm", [P, 2, 3], F32), ("rs", [P, 2, 3], F32), ("tab", [P, NMTAB], F32)])
    mg = overlay("mrg", ML0 + [("g", [P, 16, L], F32), ("r", [P, C, L], F32)] +
                 [("yh2", [P, C, L], F32R), ("yl2", [P, C, L], F32R)])

    def v(name, m=0):
        return vec[:, bass.ds(VEC[name] + m, 1)]

    def k_(name, n, rows=P):
        return con[0:rows, CON[name]:CON[name] + n]

    ident, ones = k_("ident", P), k_("ones", P)
    A = slice(META, L)
    B = slice(0, L)

    loaded = [sem(f"panel_loaded{i}") for i in range(RING)]
    start_loaded = sem("start_loaded")
    filt_loaded = sem("filt_loaded")
    panel_hi, panel_lo, panel_used = sem("panel_hi"), sem("panel_lo"), sem("panel_used")
    bank_free = sem("proj_bank_free")
    x_hi, x_lo = sem("x_hi"), sem("x_lo")
    sumsq_done, norm_total, root_ready, rinv_ready = (sem("sumsq_done"), sem("norm_total"), sem("root_ready"),
                                                      sem("rinv_ready"))
    gate_silu, hid_ready, hid_hi, hid_lo = sem("gate_silu"), sem("hid_ready"), sem("hid_hi"), sem("hid_lo")
    y_ready, y_hi, y_lo = sem("y_ready"), sem("y_hi"), sem("y_lo")
    dve_chain, act_chain, pool_chain = sem("dve_chain"), sem("act_chain"), sem("pool_chain")
    eps_set = sem("eps_set")
    filt_ps, filt_arg, filt_sin = sem("filt_ps"), sem("filt_arg"), sem("filt_sin")
    bias_loaded, bias_masked = sem("bias_loaded"), sem("bias_masked")
    na = {s: sem(f"na_{s}") for s in ("squared", "sums", "ms", "rr", "rr2", "newton", "vps", "vt", "qk", "scores",
                                      "biased", "exp", "p", "turned", "pt", "out")}
    hs = {s: sem(f"hy_{s}") for s in ("tables", "filter_in", "F", "fr", "ab", "abs", "am", "norm", "inv", "Hps", "H",
                                      "turned", "ut", "U", "Y", "back", "z")}
    re = {s: sem(f"ret_{s}") for s in ("loaded", "lg", "silu", "rot", "roped", "vps", "vt", "e", "d", "scores", "sd",
                                       "yps", "y", "centred", "squared", "var", "rr")}
    ms = {s: sem(f"mla_{s}") for s in ("loaded", "squared", "sums", "rr", "normed", "krot", "kr", "vps", "vt", "qps",
                                       "qraw", "rot", "q", "kps", "k", "scores", "max", "exp", "p", "turned0",
                                       "turned", "pt0", "pt", "out")}
    gate_on = sem("gate_on")
    out_ready, stored = sem("out_ready"), sem("stored")

    block = ctx.enter_context(nc.Block())

    def tiles_out(ph):
        return ph.t0 + ph.tiles + 4

    @block.sync
    def _(sp):
        sp.dma_start(x[:, :, A], a["xT"]).then_inc(start_loaded, 16)
        sp.dma_start(x[:, :, 0:META], a["metaT"]).then_inc(start_loaded, 16)
        sp.dma_start(vec[:], a["vec"]).then_inc(start_loaded, 16)
        sp.dma_start(con[:], a["con"]).then_inc(start_loaded, 16)
        sp.dma_start(filt_in[:], a["filt_in"]).then_inc(filt_loaded, 16)
        sp.dma_start(filt_w2[:], a["filt_w2"]).then_inc(filt_loaded, 16)

        def panels(ph, first, n):
            src, width = (a["w8"], K8 * P) if ph.k == K8 else (a["w11"], K11 * P)

            def one(i, j):
                p = ph.p0 + first + j + 4 * i
                slot = (ph.p0 + first + j) % RING
                if ph.p0 + first >= RING:
                    sp.wait_ge(panel_lo, p - RING + 1)
                sp.dma_start(raw[:, slot, 0:width], src[ph.block0 + first + j + 4 * i]).then_inc(loaded[slot], 16)

            if n >= 8:
                with sp.Fori(0, n // 4) as i:
                    for j in range(4):
                        one(i, j)
                for j in range(n % 4):
                    one(n // 4, j)
            else:
                for j in range(n):
                    one(0, j)

        for name in ORDER:
            ph = PH[name]
            if name == "in0":
                panels(ph, 0, 4)
                panels(ph, 4, 20)
            elif name == "in1":
                panels(ph, 0, 8)
                sp.wait_ge(panel_used, ph.p0)
                sp.dma_start(at["bias"][:], a["bias"]).then_inc(bias_loaded, 16)
                panels(ph, 8, 16)
            elif name == "in2":
                panels(ph, 0, 8)
                sp.wait_ge(panel_used, ph.p0)
                sp.dma_start(hy["fdft"][:], a["fdft"]).then_inc(hs["tables"], 16)
                sp.dma_start(hy["idft"][:], a["idft"]).then_inc(hs["tables"], 16)
                panels(ph, 8, 16)
            elif name == "out2":
                panels(ph, 0, 4)
                for n in range(4):
                    half, order = n // 2, n % 2
                    if n:
                        sp.wait_ge(hs["fr"], n)
                    sp.dma_start(hy["w3"][:], a["filt_w3"][:, 2 * order:2 * order + 2,
                                                          half * HC:(half + 1) * HC]).then_inc(hs["filter_in"], 16)
                    sp.dma_start(hy["decay"][:], a["decay"][:, :, half * HC:(half + 1) * HC])\
                        .then_inc(hs["filter_in"], 16)
                panels(ph, 4, 4)
            elif name == "in_ret":
                panels(ph, 0, 8)
                sp.wait_ge(panel_used, ph.p0)
                sp.dma_start(rt["tab"][:], a["ret_tab"]).then_inc(re["loaded"], 16)
                sp.dma_start(rt["dec"][:], a["decays"].broadcast_to([P, 2, RH])).then_inc(re["loaded"], 16)
                panels(ph, 8, 16)
            elif name == "in_mla":
                panels(ph, 0, 4)
                sp.wait_ge(y_lo, YBASE["ret"] + RH)
                sp.dma_start(ml["tab"][:], a["mla_tab"]).then_inc(ms["loaded"], 16)
                sp.dma_start(ml["uq"][:], a["uq"]).then_inc(ms["loaded"], 16)
                sp.dma_start(ml["uk"][:], a["uk"]).then_inc(ms["loaded"], 16)
                sp.dma_start(ml["uv"][:], a["uv"]).then_inc(ms["loaded"], 16)
                panels(ph, 4, 2)
            else:
                panels(ph, 0, ph.n)

        for m in range(C):
            sp.wait_ge(out_ready, m + 1)
            sp.dma_start(out[:, m, :], x[:, m, A]).then_inc(stored, 16)
        sp.wait_ge(stored, 16 * C)

    @block.tensor
    def _(pe):
        def panel(ph, i, j, hi, lo, cols, ready):
            slot = (ph.p0 + j) % RING
            pe.wait_ge(panel_lo, ph.p0 + j + 1 + 4 * i)
            if ph.name == "mla_out":
                groups = [(2 * j, range(4)), (2 * j + 1, range(4))]
            elif ph.k == K11:
                groups = [(j // 2, range(K11 * (j % 2), K11 * (j % 2) + K11))]
            else:
                groups = [(j, range(K8))]
            w = 0
            for tile, ks in groups:
                ps = bank[(ph.b0 + tile) % 4][:, 0:cols.stop - cols.start]
                if ph.k == K11 and j % 2 == 0:
                    pe.wait_ge(bank_free, ph.t0 + tile + 3 + 2 * i)
                elif ph.k == K8:
                    pe.wait_ge(bank_free, ph.t0 + tile + 1 + (8 if ph.name == "mla_out" else 4) * i)
                for k in ks:
                    if ready is not None and (j == 0 or (ph.k == K11 and j == 1)):
                        pe.wait_ge(ready[0], ready[1] + k + 1)
                    wc = slice(w * P, (w + 1) * P)
                    first = k == 0
                    last = k == (FC - 1 if ph.k == K11 else len(ks) - 1)
                    pe.matmul(ps, whi[:, slot, wc], hi[:, k, cols], start=first, stop=False)
                    pe.matmul(ps, whi[:, slot, wc], lo[:, k, cols], start=False, stop=False)
                    mm = pe.matmul(ps, wlo[:, slot, wc], hi[:, k, cols], start=False, stop=last)
                    w += 1
            mm.then_inc(panel_used, 1)

        def total(norm, cols):
            pe.wait_ge(sumsq_done, norm + 1)
            pe.matmul(bank[7][:, cols], ones, sumsq[:, cols], start=True, stop=True).then_inc(norm_total, 1)

        def product(name, hi, lo, cols, ready, norm=None):
            ph = PH[name]
            rounds, first = ph.n // 4, 0
            if norm is not None:
                panel(ph, 0, 0, hi, lo, cols, ready)
                total(norm, cols)
                for j in range(1, min(4, ph.n)):
                    panel(ph, 0, j, hi, lo, cols, ready)
                first = 1
            if rounds - first > 1:
                with pe.Fori(first, rounds) as i:
                    for j in range(4):
                        panel(ph, i, j, hi, lo, cols, ready)
            else:
                for i in range(first, rounds):
                    for j in range(4):
                        panel(ph, i, j, hi, lo, cols, ready)
            for j in range(ph.n % 4):
                panel2(ph, rounds, j, hi, lo, cols)

        def panel2(ph, i, j, hi, lo, cols):
            panel(ph, i, j, hi, lo, cols, None)

        def filter_hidden():
            pe.wait_ge(filt_loaded, 32)
            pe.matmul(bank[7][0:FHID, 0:SEQ], filt_in[:, SEQ:SEQ + FHID], filt_in[:, 0:SEQ], start=True,
                      stop=True).then_inc(filt_ps, 1)
            pe.wait_ge(filt_sin, 1)
            pe.matmul(bank[7][0:FHID, 0:SEQ], filt_w2[:], filt_hid[:], start=True, stop=True).then_inc(filt_ps, 1)
            pe.wait_ge(filt_arg, 2)

        def attention_in(norm):
            ph = PH["in1"]

            def head_sums(i, j, m):
                pe.wait_ge(na["squared"], m + 1)
                if j >= 2:
                    pe.wait_ge(na["ms"], m - 1)
                elif i is not None:
                    pe.wait_ge(na["ms"], m - 1)
                pe.matmul(bank[4 + j % 2][:, 0:SEQ], k_("pair_ones", P), at["sq"][:, j % 2, :], start=True,
                          stop=True).then_inc(na["sums"], 1)

            for j in range(4):
                panel(ph, 0, j, xh, xl, A, (x_lo, C * norm))
                if j == 0:
                    total(norm, A)
                if j >= 2:
                    head_sums(None, j - 2, j - 2)
            with pe.Fori(1, 4) as i:
                for j in range(4):
                    panel(ph, i, j, xh, xl, A, None)
                    head_sums(i, (j + 2) % 4, 4 * i + j - 2)
            for j in range(4):
                panel(ph, 4, j, xh, xl, A, None)
                if j < 2:
                    head_sums(4, j, 14 + j)
            for j in range(4):
                panel(ph, 5, j, xh, xl, A, None)

        def attention():
            ph = PH["in1"]
            pe.wait_ge(bank_free, tiles_out(ph))
            for t in range(NH + 5):
                if t % 2 == 0 and 2 <= t < NH + 2:
                    c = t // 2 - 1
                    if c:
                        pe.wait_ge(na["vt"], c)
                    for r in range(2):
                        mm = pe.transpose(bank[1][:, r * P:(r + 1) * P], at["qkv"][:, 16 + c, r * P:(r + 1) * P], ident)
                    mm.then_inc(na["vps"], 1)
                n = t
                if n < NH:
                    if n == 0:
                        pe.wait_ge(na["qk"], 2)
                    if n >= 2:
                        pe.wait_ge(na["biased"], n - 1)
                    rows = slice(HD * (n % 2), HD * (n % 2) + HD)
                    for r in range(2):
                        mm = pe.matmul(bank[4 + n % 2][:, r * SEQ:(r + 1) * SEQ],
                                       at["qkv"][rows, n // 2, r * P:(r + 1) * P],
                                       at["qkv"][rows, 8 + n // 2, :], start=True, stop=True)
                    mm.then_inc(na["scores"], 1)
                n = t - 2
                if 0 <= n < NH:
                    pe.wait_ge(na["p"], n + 1)
                    if n >= 2:
                        pe.wait_ge(na["pt"], n - 1)
                    for kt in range(2):
                        for r in range(2):
                            mm = pe.transpose(bank[6 + n % 2][:, kt * SEQ + r * P:kt * SEQ + (r + 1) * P],
                                              at["s"][:, n % 3, r, kt * P:(kt + 1) * P], ident)
                    mm.then_inc(na["turned"], 1)
                n = t - 4
                if 0 <= n < NH:
                    c = n // 2
                    pe.wait_ge(na["pt"], n + 1)
                    pe.wait_ge(na["vt"], c + 1)
                    if c >= 2:
                        pe.wait_ge(y_lo, YBASE["in1"] + c - 1)
                    rows = slice(HD * (n % 2), HD * (n % 2) + HD)
                    for kt in range(2):
                        mm = pe.matmul(bank[2 + c % 2][rows, 0:SEQ], at["vt"][:, c % 2, kt, rows],
                                       at["pt"][:, n % 2, kt, :], start=kt == 0, stop=kt == 1)
                    mm.then_inc(na["out"], 1)
            pe.wait_ge(y_lo, YBASE["in1"] + C)

        def hyena():
            pe.wait_ge(bank_free, tiles_out(PH["in2"]))
            pe.wait_ge(hs["tables"], 32)
            for n in range(4):
                half = n // 2
                pe.wait_ge(hs["filter_in"], 32 * (n + 1))
                if n:
                    pe.wait_ge(hs["Y"], n)
                for d in range(2):
                    for r in range(2):
                        mm = pe.matmul(bank[4 + 2 * d + r][:], filt_hid[:, r * P:(r + 1) * P], hy["w3"][:, d, :],
                                       start=True, stop=True)
                mm.then_inc(hs["F"], 1)
                pe.wait_ge(hs["ab"], n + 1)
                if n:
                    pe.wait_ge(hs["z"], 4 * n)
                for i, (part, col) in enumerate(((0, 0), (0, P), (1, SEQ), (1, SEQ + P), (0, 2 * SEQ))):
                    if i == 3:
                        pe.wait_ge(hs["H"], 5 * n + 1)
                    if i == 4:
                        pe.wait_ge(hs["H"], 5 * n + 2)
                    for r in range(2):
                        mm = pe.matmul(bank[1 + i % 3][:], hy["fdft"][:, r, col:col + P], hy["ab"][:, part, r, :],
                                       start=r == 0, stop=r == 1)
                    mm.then_inc(hs["Hps"], 1)
                pe.wait_ge(hs["am"], n + 1)
                for j in range(HJ):
                    for r in range(2):
                        mm = pe.matmul(bank[0][:, j:j + 1], hy["am"][:, r, j * P:(j + 1) * P], ones[:, 0:1],
                                       start=r == 0, stop=r == 1)
                mm.then_inc(hs["norm"], 1)
                pe.wait_ge(hs["inv"], n + 1)
                pe.wait_ge(hs["H"], 5 * n + 3)
                for r in range(2):
                    for j in range(HJ):
                        mm = pe.transpose(bank[3 * r][:, j * P:(j + 1) * P],
                                          hy["z"][:, half * HJ + j, r * P:(r + 1) * P], ident)
                mm.then_inc(hs["turned"], 1)
                pe.wait_ge(hs["ut"], n + 1)
                pe.wait_ge(hs["fr"], n + 1)
                for i, col in enumerate((0, P, SEQ, SEQ + P)):
                    for r in range(2):
                        mm = pe.matmul(bank[4 + i][:], hy["fdft"][:, r, col:col + P], hy["ut"][:, r, :],
                                       start=r == 0, stop=r == 1)
                mm.then_inc(hs["U"], 1)
                pe.wait_ge(hs["Y"], n + 1)
                for j in range(HJ):
                    for i in range(4):
                        mm = pe.matmul(bank[j][:, 0:SEQ], hy["frY"][:, i, j * P:(j + 1) * P], hy["idft"][:, i, :],
                                       start=i == 0, stop=i == 3)
                    mm.then_inc(hs["back"], 1)
            pe.wait_ge(y_lo, YBASE["in2"] + C)

        def retention():
            pe.wait_ge(bank_free, tiles_out(PH["in_ret"]))
            pe.wait_ge(re["loaded"], 32)
            rot = rt["tab"][:, RTAB["rot"]:RTAB["rot"] + P]
            centre = rt["tab"][:, RTAB["center"]:RTAB["center"] + P]
            for i in range(8):
                if i >= 2:
                    pe.wait_ge(re["roped"], i - 1)
                pe.matmul(bank[4 + i % 2][:, B], rot, rt["t"][:, i, :], start=True, stop=True).then_inc(re["rot"], 1)
                if i >= 2:
                    pe.wait_ge(re["vt"], i - 1)
                for r, (t0, tn) in enumerate(JT):
                    mm = pe.transpose(bank[6 + i % 2][0:tn, r * P:(r + 1) * P], rt["t"][:, 8 + i, t0:t0 + tn], ident)
                mm.then_inc(re["vps"], 1)
            pe.wait_ge(re["roped"], 8)
            pe.wait_ge(re["vt"], 8)
            for t in range(RH + 3):
                h = t
                if h < RH:
                    rows = slice(RDK * (h % 2), RDK * (h % 2) + RDK)
                    if h:
                        pe.wait_ge(re["sd"], h)
                    for r, (t0, tn) in enumerate(JT):
                        mm = pe.matmul(bank[r][0:tn, B], rt["t"][rows, 4 + h // 2, t0:t0 + tn],
                                       rt["t"][rows, h // 2, :], start=True, stop=True)
                    mm.then_inc(re["scores"], 1)
                h = t - 1
                if 0 <= h < RH:
                    pe.wait_ge(re["sd"], h + 1)
                    if h:
                        pe.wait_ge(re["y"], h)
                    for r, (t0, tn) in enumerate(JT):
                        mm = pe.matmul(bank[3][:, B], rt["vt"][0:tn, r, h * P:(h + 1) * P],
                                       rt["sd"][0:tn, h % 2, r, :], start=r == 0, stop=r == 2)
                    mm.then_inc(re["yps"], 1)
                h = t - 2
                if 0 <= h < RH:
                    pe.wait_ge(re["y"], h + 1)
                    if h >= 2:
                        pe.wait_ge(y_ready, YR["ret"] + h - 1)
                    pe.matmul(bank[4 + h % 2][:, B], centre, rt["y"][:], start=True,
                              stop=True).then_inc(re["centred"], 1)
                h = t - 3
                if 0 <= h < RH:
                    pe.wait_ge(re["squared"], h + 1)
                    if h:
                        pe.wait_ge(re["rr"], h)
                    pe.matmul(bank[6][:, B], ones, rt["sq"][:], start=True, stop=True).then_inc(re["var"], 1)
            pe.wait_ge(y_lo, YBASE["ret"] + RH)

        def latent():
            pe.wait_ge(bank_free, tiles_out(PH["in_mla"]))
            pe.wait_ge(ms["loaded"], 64)
            rot = ml["tab"][0:MQK, MTAB["rot"]:MTAB["rot"] + MQK]
            for g, (c0, cn) in enumerate(((0, QR // P), (QR // P, KR // P))):
                pe.wait_ge(ms["squared"], g + 1)
                for i in range(cn):
                    mm = pe.matmul(bank[4 + g][:, B], ones, ml["sq"][:, i, :], start=i == 0, stop=i == cn - 1)
                mm.then_inc(ms["sums"], 1)
            pe.matmul(bank[6][0:MQK, B], rot, ml["c"][0:MQK, 5, :], start=True, stop=True).then_inc(ms["krot"], 1)
            pe.wait_ge(ms["normed"], 2)
            for r, (t0, tn) in enumerate(JT):
                for i in range(2):
                    mm = pe.matmul(bank[r][0:tn, :], ml["c"][:, 3 + i, t0:t0 + tn], ml["uv"][:, i, :],
                                   start=i == 0, stop=i == 1)
                mm.then_inc(ms["vps"], 1)
            pe.wait_ge(ms["vt"], 3)
            pe.wait_ge(ms["kr"], 1)
            for t in range(MH + 3):
                h = t
                if h < MH:
                    if h:
                        pe.wait_ge(ms["k"], h)
                    for i in range(3):
                        mm = pe.matmul(bank[0][0:MQK, B], ml["uq"][:, i, h * MQK:(h + 1) * MQK], ml["c"][:, i, :],
                                       start=i == 0, stop=i == 2)
                    mm.then_inc(ms["qps"], 1)
                    pe.wait_ge(ms["qraw"], h + 1)
                    if h:
                        pe.wait_ge(ms["q"], h)
                    pe.matmul(bank[1][0:MQK, B], rot, ml["qraw"][0:MQK, :], start=True,
                              stop=True).then_inc(ms["rot"], 1)
                    for i in range(2):
                        mm = pe.matmul(bank[0][0:NOPE, B], ml["uk"][:, i, h * NOPE:(h + 1) * NOPE],
                                       ml["c"][:, 3 + i, :], start=i == 0, stop=i == 1)
                    mm.then_inc(ms["kps"], 1)
                h = t - 3
                if 0 <= h < MH:
                    pe.wait_ge(ms["pt"], h + 1)
                    if h >= 2 and h % 2 == 0:
                        pe.wait_ge(y_lo, YBASE["mla"] + h // 2)
                    rows = slice(MDV * (h % 2), MDV * (h % 2) + MDV)
                    for r, (t0, tn) in enumerate(JT):
                        mm = pe.matmul(bank[2][rows, B], ml["vt"][0:tn, r, h * MDV:(h + 1) * MDV],
                                       ml["pt"][0:tn, r, :], start=r == 0, stop=r == 2)
                    mm.then_inc(ms["out"], 1)
                h = t - 1
                if 0 <= h < MH:
                    pe.wait_ge(ms["q"], h + 1)
                    pe.wait_ge(ms["k"], h + 1)
                    if h:
                        pe.wait_ge(ms["exp"], h)
                    for r, (t0, tn) in enumerate(JT):
                        mm = pe.matmul(bank[3 + r][0:tn, B], ml["q"][0:MQK, h % 2, t0:t0 + tn],
                                       ml["k"][0:MQK, h % 2, :], start=True, stop=True)
                    mm.then_inc(ms["scores"], 1)
                h = t - 2
                if 0 <= h < MH:
                    pe.wait_ge(ms["p"], h + 1)
                    for r, (t0, tn) in enumerate(JT):
                        if r == 2:
                            pe.wait_ge(ms["pt0"], h + 1)
                        elif h:
                            pe.wait_ge(ms["pt"], h)
                        for q, (q0, qn) in enumerate(JT):
                            mm = pe.transpose(bank[6 + r % 2][0:tn, q0:q0 + qn], ml["s"][0:qn, h % 2, q, t0:t0 + tn],
                                              k_("ident", P)[0:qn, 0:qn])
                        mm.then_inc(ms["turned"], 1)
            pe.wait_ge(y_lo, YBASE["mla"] + 4)

        pe.wait_ge(start_loaded, 64)
        filter_hidden()
        norm = 0
        for layer, kind in enumerate(KINDS):
            if kind == "attention":
                attention_in(norm)
                attention()
            else:
                product(f"in{layer}", xh, xl, A, (x_lo, C * norm), norm)
            norm += 1
            if kind == "hyena":
                hyena()
            bufs = {"conv": cm, "attention": at, "hyena": hy}[kind]
            product(f"out{layer}", bufs["yh"], bufs["yl"], A, (y_lo, YBASE[f"in{layer}"]))
            product(f"up{layer}", xh, xl, A, (x_lo, C * norm), norm)
            norm += 1
            product(f"down{layer}", ffn["hh"], ffn["hl"], A, (hid_lo, FC * layer))
        product("in_ret", xh, xl, B, (x_lo, C * norm), norm)
        norm += 1
        retention()
        product("in_mla", xh, xl, B, None)
        latent()
        product("in_gate", xh, xl, B, None)
        product("ret_out", rt["yh"], rt["yl"], B, None)
        product("mla_out", ml["yh"], ml["yl"], B, None)
        product("w_o", mg["yh2"], mg["yl2"], B, (y_lo, YBASE["mrg"]))
        product("up4", xh, xl, B, (x_lo, C * norm), norm)
        norm += 1
        product("down4", ffn["hh"], ffn["hl"], B, (hid_lo, FC * DEPTH))
        pe.wait_ge(sumsq_done, norm + 1)
        pe.matmul(bank[7][:, B], ones, sumsq[:], start=True, stop=True).then_inc(norm_total, 1)
        assert norm + 1 == NORMS

    def steps(eng, ph, first, n, step, chain=None, per=0, ahead=4):
        crossing = first + n == ph.n and ph.next_k != ph.k
        rounds = n // 4 - (1 if crossing else 0)

        def one(i, j, split):
            step(i, j, split)

        if rounds > 1:
            start = chain.n if chain else 0
            with eng.Fori(0, rounds) as i:
                if chain:
                    chain.n = start + i * per
                for j in range(4):
                    one(i, j, ph.k)
            if chain:
                chain.n = start + rounds * per
        else:
            for i in range(rounds):
                for j in range(4):
                    one(i, j, ph.k)
        for i in range(rounds, n // 4):
            for j in range(4):
                one(i, j, ph.next_k if j + ahead >= 4 else ph.k)
        for j in range(n % 4):
            one(n // 4, j, ph.k)

    @block.scalar
    def _(act):
        link = Chain(act, act_chain)

        def split_hi(ph, first, i, j, k):
            if k is None:
                return
            p = ph.p0 + first + j
            act.wait_ge(loaded[p % RING], 16 * (p // RING + 2) + 16 * i)
            act.wait_ge(panel_used, p + 1 + 4 * i)
            nc.scalar.copy(whi[:, p % RING, 0:k * P], raw[:, p % RING, 0:k * P]).then_inc(panel_hi, 1)

        def norm_root(norm, cols):
            act.wait_ge(norm_total, norm + 1)
            nc.scalar.activation(root[:, cols], bank[7][:, cols], ACT.Sqrt, bias=eps[:, 0:1],
                                 scale=1.0 / D).then_inc(root_ready, 1)

        def only_split(ph, first=0, n=None):
            def step(i, j, k):
                split_hi(ph, first, i, j, k)
            steps(act, ph, first, ph.n if n is None else n, step)

        def gates(ph, ffn_index, cols):
            w = slice(0, cols.stop - cols.start)
            g0 = ffn_index * FC

            def step(i, j, k):
                s = j // 2
                split_hi(ph, 0, i, j, k)
                if j % 2 == 0:
                    act.wait_ge(bank_free, ph.t0 + j + 5 + 4 * i)
                    nc.scalar.activation(silu[:, s, w], gate[:, s, w], ACT.Silu).then_inc(gate_silu, 1)
                else:
                    act.wait_ge(hid_ready, g0 + s + 1 + 2 * i)
                    nc.scalar.copy(ffn["hh"][:, s + 2 * i, cols], hid[:, s, w]).then_inc(hid_hi, 1)
            steps(act, ph, 0, ph.n, step)

        def y_high(ph, first, n, dst, cols, ready0):
            w = slice(0, cols.stop - cols.start)

            def step(i, j, k):
                split_hi(ph, first, i, j, k)
                act.wait_ge(y_ready, ready0 + j + 1 + 4 * i)
                nc.scalar.copy(dst[:, j + 4 * i, cols], hid[:, j % 2, w]).then_inc(y_hi, 1)
            steps(act, ph, first, n, step)

        def attention():
            ph = PH["in1"]

            def squares(i, j, k):
                m = j + 4 * i
                split_hi(ph, 0, i, j, k)
                act.wait_ge(bank_free, ph.t0 + j + 5 + 4 * i)
                if not (isinstance(i, int) and m < 2):
                    act.wait_ge(na["sums"], m - 1)
                    nc.scalar.activation(an["ms"][:, m - 2, :], bank[4 + j % 2][:, 0:SEQ], ACT.Identity,
                                         bias=eps[:, 0:1], scale=1.0 / HD).then_inc(na["ms"], 1)
                nc.scalar.activation(at["sq"][:, j % 2, :], at["qkv"][:, m, :], ACT.Square).then_inc(na["squared"], 1)

            for j in range(4):
                squares(0, j, K8)
            with act.Fori(1, 4) as i:
                for j in range(4):
                    squares(i, j, K8)
            for m in (14, 15):
                act.wait_ge(na["sums"], m + 1)
                nc.scalar.activation(an["ms"][:, m, :], bank[4 + m % 2][:, 0:SEQ], ACT.Identity,
                                     bias=eps[:, 0:1], scale=1.0 / HD).then_inc(na["ms"], 1)

            def split(j):
                split_hi(ph, 16, 0, j, K8)

            split(0)
            act.wait_ge(na["ms"], 16)
            link(nc.scalar.activation(an["rr"][:], an["ms"][:], ACT.Ln))
            split(1)
            nc.scalar.activation(an["rr"][:], an["rr"][:], ACT.Exp, scale=-0.5).then_inc(na["rr"], 1)
            act.wait_ge(na["rr"], 1)
            for g in range(4):
                if g:
                    act.wait_ge(na["newton"], g)
                nc.scalar.activation(an["nw"][:], an["rr"][:, 4 * g:4 * g + 4, :], ACT.Square).then_inc(na["rr2"], 1)
                split(2 + g)
            split(6)
            split(7)
            act.wait_ge(na["qk"], 2)
            for t in range(NH + 4):
                if t % 2 == 0 and 2 <= t < NH + 2:
                    c = t // 2 - 1
                    act.wait_ge(na["vps"], c + 1)
                    if c >= 2:
                        act.wait_ge(na["out"], 2 * c - 2)
                    nc.scalar.copy(at["vt"][:, c % 2].rearrange("p a b -> p (a b)"),
                                   bank[1][:, 0:2 * P]).then_inc(na["vt"], 1)
                n = t
                if 0 <= n < NH:
                    act.wait_ge(na["biased"], n + 1)
                    for r in range(2):
                        e = nc.scalar.activation(at["s"][:, n % 3, r, :], at["s"][:, n % 3, r, :], ACT.Exp,
                                                 bias=at["mx"][:, n % 3, r:r + 1],
                                                 accum_out=at["sm"][:, n % 3, r:r + 1])
                    e.then_inc(na["exp"], 1)
                n = t - 3
                if 0 <= n < NH:
                    act.wait_ge(na["turned"], n + 1)
                    if n >= 2:
                        act.wait_ge(na["out"], n - 1)
                    nc.scalar.copy(at["pt"][:, n % 2].rearrange("p a b -> p (a b)"),
                                   bank[6 + n % 2][:]).then_inc(na["pt"], 1)

        def hyena():
            for n in range(4):
                act.wait_ge(hs["ab"], n + 1)
                for part in range(2):
                    ab = nc.scalar.activation(hy["H"][:, 2 * part:2 * part + 2, :], hy["ab"][:, part], ACT.Abs)
                ab.then_inc(hs["abs"], 1)
                act.wait_ge(hs["am"], n + 1)
                for i in range(5):
                    act.wait_ge(hs["Hps"], 5 * n + i + 1)
                    nc.scalar.copy(hy["H"][:, i, :], bank[1 + i % 3][:]).then_inc(hs["H"], 1)
                act.wait_ge(hs["turned"], n + 1)
                nc.scalar.copy(hy["ut"][:, 0, :], bank[0][:])
                nc.scalar.copy(hy["ut"][:, 1, :], bank[3][:]).then_inc(hs["ut"], 1)

        def retention():
            act.wait_ge(bank_free, tiles_out(PH["in_ret"]))
            act.wait_ge(re["loaded"], 32)
            for m in range(8):
                nc.scalar.activation(rt["t"][:, 16 + m, :], rt["t"][:, 16 + m, :], ACT.Silu).then_inc(re["silu"], 1)
            for i in range(8):
                act.wait_ge(re["vps"], i + 1)
                nc.scalar.copy(rt["vt"][:, 0:2, i * P:(i + 1) * P],
                               bank[6 + i % 2][:, 0:2 * P].rearrange("p (a b) -> p a b", a=2))
                nc.scalar.copy(rt["vt"][0:JT[2][1], 2, i * P:(i + 1) * P],
                               bank[6 + i % 2][0:JT[2][1], 2 * P:3 * P]).then_inc(re["vt"], 1)
            nc.scalar.activation(rt["lg"][:], rt["dec"][:], ACT.Exp).then_inc(re["lg"], 1)
            act.wait_ge(re["lg"], 2)
            back = rt["tab"][:, RTAB["back"]:RTAB["back"] + 3 * L]
            ahead = rt["tab"][:, RTAB["ahead"]:RTAB["ahead"] + 3 * L]

            def decay(h):
                if h >= 2:
                    act.wait_ge(re["sd"], h - 1)
                nc.scalar.activation(rt["e1"][:, h % 2].rearrange("p a b -> p (a b)"), back, ACT.Exp,
                                     scale=rt["lg"][:, 0, h:h + 1])
                if h:
                    act.wait_ge(re["d"], h)
                nc.scalar.activation(rt["e2"][:].rearrange("p a b -> p (a b)"), ahead, ACT.Exp,
                                     scale=rt["lg"][:, 1, h:h + 1]).then_inc(re["e"], 1)

            decay(0)
            for t in range(RH + 3):
                if t + 1 < RH:
                    decay(t + 1)
                h = t - 1
                if 0 <= h < RH:
                    act.wait_ge(re["yps"], h + 1)
                    if h:
                        act.wait_ge(re["centred"], h)
                    nc.scalar.copy(rt["y"][:], bank[3][:, B]).then_inc(re["y"], 1)
                h = t - 2
                if 0 <= h < RH:
                    act.wait_ge(re["centred"], h + 1)
                    if h:
                        act.wait_ge(re["var"], h)
                    nc.scalar.activation(rt["sq"][:], bank[4 + h % 2][:, B], ACT.Square).then_inc(re["squared"], 1)
                h = t - 3
                if 0 <= h < RH:
                    act.wait_ge(re["var"], h + 1)
                    if h:
                        act.wait_ge(y_ready, YR["ret"] + h)
                    link(nc.scalar.activation(rt["rr"][:], bank[6][:, B], ACT.Ln, bias=eps[:, 1:2], scale=1.0 / RDV))
                    nc.scalar.activation(rt["rr"][:], rt["rr"][:], ACT.Exp, scale=-0.5).then_inc(re["rr"], 1)

        def latent():
            act.wait_ge(bank_free, tiles_out(PH["in_mla"]))
            act.wait_ge(ms["loaded"], 64)
            for g, (c0, cn) in enumerate(((0, QR // P), (QR // P, KR // P))):
                if g:
                    act.wait_ge(ms["sums"], 1)
                nc.scalar.activation(ml["sq"][:, 0:cn, :], ml["c"][:, c0:c0 + cn, :],
                                     ACT.Square).then_inc(ms["squared"], 1)
                act.wait_ge(ms["sums"], g + 1)
                link(nc.scalar.activation(ml["rr"][:, g, :], bank[4 + g][:, B], ACT.Ln, bias=eps[:, 0:1],
                                          scale=1.0 / (cn * P)))
                nc.scalar.activation(ml["rr"][:, g, :], ml["rr"][:, g, :], ACT.Exp, scale=-0.5).then_inc(ms["rr"], 1)
            for r, (t0, tn) in enumerate(JT):
                act.wait_ge(ms["vps"], r + 1)
                nc.scalar.copy(ml["vt"][0:tn, r, :], bank[r][0:tn, :]).then_inc(ms["vt"], 1)
            act.wait_ge(ms["kr"], 1)
            for t in range(MH + 2):
                h = t
                if h < MH:
                    act.wait_ge(ms["qps"], h + 1)
                    if h:
                        act.wait_ge(ms["q"], h)
                    nc.scalar.copy(ml["qraw"][0:MQK, :], bank[0][0:MQK, B]).then_inc(ms["qraw"], 1)
                    act.wait_ge(ms["kps"], h + 1)
                    if h >= 2:
                        act.wait_ge(ms["scores"], h - 1)
                    nc.scalar.copy(ml["k"][NOPE:MQK, h % 2, :], ml["kr"][NOPE:MQK, :])
                    nc.scalar.copy(ml["k"][0:NOPE, h % 2, :], bank[0][0:NOPE, B]).then_inc(ms["k"], 1)
                h = t - 2
                if 0 <= h < MH:
                    if h:
                        act.wait_ge(ms["out"], h)
                    for r, (t0, tn) in enumerate(JT):
                        act.wait_ge(ms["turned"], 3 * h + r + 1)
                        e = nc.scalar.copy(ml["pt"][0:tn, r, :], bank[6 + r % 2][0:tn, B])
                        if r == 0:
                            e.then_inc(ms["pt0"], 1)
                    e.then_inc(ms["pt"], 1)
                h = t - 1
                if 0 <= h < MH:
                    act.wait_ge(ms["max"], h + 1)
                    if h >= 2:
                        act.wait_ge(ms["turned"], 3 * (h - 1))
                    for r, (t0, tn) in enumerate(JT):
                        e = nc.scalar.activation(ml["s"][0:tn, h % 2, r, :], bank[3 + r][0:tn, B], ACT.Exp,
                                                 bias=ml["mx"][0:tn, h % 2, r:r + 1], scale=MQK ** -0.5,
                                                 accum_out=ml["sm"][0:tn, h % 2, r:r + 1])
                    e.then_inc(ms["exp"], 1)

        act.wait_ge(eps_set, 1)
        act.wait_ge(filt_arg, 1)
        nc.scalar.activation(filt_hid[:], filt_x[:], ACT.Sin).then_inc(filt_sin, 1)
        for p in range(RING):
            act.wait_ge(loaded[p], 16)
            nc.scalar.copy(whi[:, p, 0:K8 * P], raw[:, p, 0:K8 * P]).then_inc(panel_hi, 1)
        act.wait_ge(filt_arg, 2)
        nc.scalar.activation(filt_hid[:], filt_x[:], ACT.Sin).then_inc(filt_sin, 1)
        norm = 0
        for layer, kind in enumerate(KINDS):
            ph = PH[f"in{layer}"]
            norm_root(norm, A)
            norm += 1
            if kind == "conv":
                only_split(ph, 0, 16)
                y_high(ph, 16, 8, cm["yh"], A, YR[f"in{layer}"])
            elif kind == "attention":
                attention()
            else:
                only_split(ph)
                hyena()
            only_split(PH[f"out{layer}"])
            norm_root(norm, A)
            norm += 1
            gates(PH[f"up{layer}"], layer, A)
            only_split(PH[f"down{layer}"])
        norm_root(norm, B)
        norm += 1
        only_split(PH["in_ret"])
        retention()
        only_split(PH["in_mla"])
        latent()

        ph_gate = PH["in_gate"]

        def gate_step(i, j, k):
            split_hi(ph_gate, 0, i, j, k)
            act.wait_ge(bank_free, ph_gate.t0 + j + 5 + 4 * i)
            g = mg["g"][:, j + 4 * i, :]
            nc.scalar.activation(g, g, ACT.Sigmoid).then_inc(gate_on, 1)
        steps(act, ph_gate, 0, 16, gate_step)
        only_split(PH["ret_out"])

        ph_mo = PH["mla_out"]
        for j in range(4):
            for u in range(2):
                m = 2 * j + u
                act.wait_ge(y_ready, YR["mrg"] + m + 1)
                nc.scalar.copy(mg["yh2"][:, m, :], hid[:, u, :]).then_inc(y_hi, 1)
            split_hi(ph_mo, 0, 0, j, K8)
        only_split(PH["w_o"])
        norm_root(norm, B)
        norm += 1
        gates(PH["up4"], DEPTH, B)
        only_split(PH["down4"])
        norm_root(norm, B)

    @block.gpsimd
    def _(pool):
        link = Chain(pool, pool_chain)
        pool.wait_ge(start_loaded, 64)

        def decay_products():
            for h in range(RH):
                pool.wait_ge(re["e"], h + 1)
                e1 = rt["e1"][:, h % 2].rearrange("p a b -> p (a b)")
                nc.gpsimd.tensor_tensor(e1, e1, rt["e2"][:].rearrange("p a b -> p (a b)"),
                                        ALU.mult).then_inc(re["d"], 1)

        for norm in range(NORMS):
            cols = A if norm < 2 * DEPTH else B
            if norm == 2 * DEPTH + 1:
                decay_products()
            if norm == NORMS - 1:
                s, base = bank_free, PH["down4"].t0 + 4
            else:
                s, base = x_hi, C * norm
            pool.wait_ge(s, base + 1)
            link(nc.gpsimd.tensor_tensor(sumsq[:, cols], x[:, 0, cols], x[:, 0, cols], ALU.mult))
            start = link.n
            with pool.Fori(1, C) as m:
                link.n = start + 2 * (m - 1)
                pool.wait_ge(s, base + 1 + m)
                link(nc.gpsimd.tensor_tensor(square[:, cols], x[:, m, cols], x[:, m, cols], ALU.mult))
                link(nc.gpsimd.tensor_tensor(sumsq[:, cols], sumsq[:, cols], square[:, cols], ALU.add))
            link.n = start + 2 * (C - 1)
            nc.gpsimd.memset(square[:, 0:2], 0.0).then_inc(sumsq_done, 1)

    def dve_steps(*args):
        steps(nc.vector, *args, ahead=3)

    @block.vector
    def _(dve):
        link = Chain(dve, dve_chain)
        V = nc.vector

        def split_lo(ph, first, i, j, k):
            if k is None:
                return
            p = ph.p0 + first + j + 3
            dve.wait_ge(panel_hi, p + 1 + 4 * i)
            V.tensor_tensor(wlo[:, p % RING, 0:k * P], raw[:, p % RING, 0:k * P],
                            whi[:, p % RING, 0:k * P].bitcast(F32), ALU.subtract).then_inc(panel_lo, 1)

        def norm_inv(norm, cols):
            dve.wait_ge(root_ready, norm + 1)
            V.tensor_scalar(mean_sq[:, cols], bank[7][:, cols], 1.0 / D, EPS, ALU.mult, ALU.add)
            link(V.reciprocal(rinv[:, cols], root[:, cols]))
            link(V.tensor_tensor(newton[:, cols], rinv[:, cols], rinv[:, cols], ALU.mult))
            link(V.tensor_tensor(newton[:, cols], newton[:, cols], mean_sq[:, cols], ALU.mult))
            link(V.tensor_scalar(newton[:, cols], newton[:, cols], -0.5, 1.5, ALU.mult, ALU.add))
            V.tensor_tensor(rinv[:, cols], rinv[:, cols], newton[:, cols], ALU.mult).then_inc(rinv_ready, 1)
            dve.wait_ge(rinv_ready, norm + 1)

        def x_parts(m, gain, cols, norm):
            V.tensor_scalar(xh[:, m, cols], x[:, m, cols], gain, None, ALU.mult).then_inc(x_hi, 1)
            dve.wait_ge(x_hi, C * norm + m + 1)
            V.scalar_tensor_tensor(out=xl[:, m, cols], in0=x[:, m, cols], scalar=gain,
                                   in1=xh[:, m, cols].bitcast(F32), op0=ALU.mult,
                                   op1=ALU.subtract).then_inc(x_lo, 1)

        def residual(ph, gain, cols, norm, next_cols):
            w = slice(0, cols.stop - cols.start)

            def step(i, j, k):
                half = ph.k == K11
                m = j // 2 + 2 * i if half else j + 4 * i
                tile = (ph.t0 + (j // 2 if half else j)) - ph.t0
                if not half or j % 2:
                    dve.wait_ge(panel_used, ph.p0 + j + 1 + 4 * i)
                    V.tensor_tensor(x[:, m, cols], x[:, m, cols], bank[(ph.b0 + tile) % 4][:, w],
                                    ALU.add).then_inc(bank_free, 1)
                    if norm < NORMS - 1:
                        dve.wait_ge(bank_free, ph.t0 + m + 5)
                        x_parts(m, v(gain[0], gain[1] + m), next_cols, norm)
                split_lo(ph, 0, i, j, k)
            dve_steps(ph, 0, ph.n, step)

        def scaled(ph, first, n, dst, keep=None):
            def step(i, j, k):
                m = j + 4 * i
                t = ph.t0 + first + j
                dve.wait_ge(panel_used, ph.p0 + first + j + 1 + 4 * i)
                d = dst(j, m)
                cols = A if d.shape[-1] == SEQ else B
                V.tensor_tensor(d, bank[(ph.b0 + first + j) % 4][:, 0:d.shape[-1]], rinv[:, cols],
                                ALU.mult).then_inc(bank_free, 1)
                if keep is not None:
                    dve.wait_ge(bank_free, t + 5 + 4 * i)
                    keep(j, m)
                split_lo(ph, first, i, j, k)
            return step

        def feed_forward(ph, index, cols):
            w = slice(0, cols.stop - cols.start)
            g0 = index * FC

            def low(i, s):
                dve.wait_ge(hid_hi, g0 + s + 1 + 2 * i)
                V.tensor_tensor(ffn["hl"][:, s + 2 * i, cols], hid[:, s, w],
                                ffn["hh"][:, s + 2 * i, cols].bitcast(F32), ALU.subtract).then_inc(hid_lo, 1)

            def step(i, j, k):
                s = j // 2
                dve.wait_ge(panel_used, ph.p0 + j + 1 + 4 * i)
                ps = bank[(ph.b0 + j) % 4][:, w]
                if j % 2 == 0:
                    V.tensor_tensor(gate[:, s, w], ps, rinv[:, cols], ALU.mult).then_inc(bank_free, 1)
                    split_lo(ph, 0, i, j, k)
                    if j == 2:
                        low(i, 0)
                    return
                V.tensor_tensor(up[:, s, w], ps, rinv[:, cols], ALU.mult).then_inc(bank_free, 1)
                dve.wait_ge(bank_free, ph.t0 + j + 5 + 4 * i)
                dve.wait_ge(gate_silu, g0 + s + 1 + 2 * i)
                V.tensor_tensor(hid[:, s, w], silu[:, s, w], up[:, s, w], ALU.mult).then_inc(hid_ready, 1)
                split_lo(ph, 0, i, j, k)
                if j == 3:
                    low(i, 1)
            dve_steps(ph, 0, ph.n, step)

        def short_conv(layer):
            ph, ai = PH[f"in{layer}"], layer // 3
            if layer == 0:
                pass
            link(V.memset(cm["cu"][:], 0.0))
            dve_steps(ph, 0, 8, scaled(ph, 0, 8, lambda j, m: cm["c"][:, m, :]))

            def taps(j, m):
                cu, cv = cm["cu"][:, j % 2], cm["cv"][:, m, :]
                w = VEC["a_conv"] + ai * 3 * C
                col = [vec[:, bass.ds(w + t * C + m, 1)] for t in range(3)]
                link(V.tensor_tensor(cu[:, 1:SEQ + 1], up[:, j % 2, 0:SEQ], cm["c"][:, m, :], ALU.mult))
                link(V.tensor_scalar(cv, cu[:, 0:SEQ], col[0], None, ALU.mult))
                for t in (1, 2):
                    link(V.scalar_tensor_tensor(out=cv, in0=cu[:, t:t + SEQ], scalar=col[t], in1=cv, op0=ALU.mult,
                                                op1=ALU.add))
            dve_steps(ph, 8, 8, scaled(ph, 8, 8, lambda j, m: up[:, j % 2, 0:SEQ], taps), link, 16)

            ready0, y0 = YR[f"in{layer}"], YBASE[f"in{layer}"]

            def step(i, j, k):
                m = j + 4 * i
                dve.wait_ge(panel_used, ph.p0 + 16 + j + 1 + 4 * i)
                V.tensor_tensor(up[:, j % 2, 0:SEQ], bank[(ph.b0 + j) % 4][:, 0:SEQ], rinv[:, A],
                                ALU.mult).then_inc(bank_free, 1)
                dve.wait_ge(bank_free, ph.t0 + 16 + j + 5 + 4 * i)
                V.tensor_tensor(hid[:, j % 2, 0:SEQ], up[:, j % 2, 0:SEQ], cm["cv"][:, m, :],
                                ALU.mult).then_inc(y_ready, 1)
                split_lo(ph, 16, i, j, k)
                dve.wait_ge(y_hi, y0 + m + 1)
                V.tensor_tensor(cm["yl"][:, m, A], hid[:, j % 2, 0:SEQ], cm["yh"][:, m, A].bitcast(F32),
                                ALU.subtract).then_inc(y_lo, 1)
            dve_steps(ph, 16, 8, step)

        def y_from_bank(bufs, c, ps, cols, y0):
            V.tensor_copy(bufs["yh"][:, c, cols], ps).then_inc(y_hi, 1)
            dve.wait_ge(y_hi, y0 + c + 1)
            V.tensor_tensor(bufs["yl"][:, c, cols], ps, bufs["yh"][:, c, cols].bitcast(F32),
                            ALU.subtract).then_inc(y_lo, 1)

        def attention():
            ph = PH["in1"]
            dve_steps(ph, 0, 16, scaled(ph, 0, 16, lambda j, m: at["qkv"][:, m, :]))
            value = scaled(ph, 16, 8, lambda j, m: at["qkv"][:, 16 + m, :])
            value(0, 0, K8)
            dve.wait_ge(bias_loaded, 16)
            bias = at["bias"][:].rearrange("p h j k -> p (h j) k")
            mask = k_("colmask", GW).unsqueeze(1).broadcast_to([P, NH * 6, GW])
            V.tensor_tensor(bias, bias, mask, ALU.add).then_inc(bias_masked, 1)
            value(0, 1, K8)
            value(0, 2, K8)
            for g in range(4):
                value(0 if g == 0 else 1, (3 + g) % 4, K8)
                dve.wait_ge(na["rr2"], g + 1)
                rr = an["rr"][:, 4 * g:4 * g + 4, :]
                link(V.tensor_tensor(an["nw"][:], an["nw"][:], an["ms"][:, 4 * g:4 * g + 4, :], ALU.mult))
                V.scalar_tensor_tensor(out=rr, in0=an["nw"][:], scalar=-3.0, in1=rr, op0=ALU.add,
                                       op1=ALU.mult).then_inc(na["newton"], 1)
            value(1, 3, K8)
            dve.wait_ge(na["newton"], 4)
            for s, g in enumerate(("q_g", "k_g")):
                qk = at["qkv"][:, 8 * s:8 * s + 8, :]
                V.scalar_tensor_tensor(out=qk, in0=qk, scalar=v(g), in1=an["rr"][:, 8 * s:8 * s + 8, :],
                                       op0=ALU.mult, op1=ALU.mult).then_inc(na["qk"], 1)
            dve.wait_ge(bias_masked, 1)
            dve.wait_ge(na["qk"], 2)
            for t in range(NH + 6):
                n = t
                if 0 <= n < NH:
                    dve.wait_ge(na["scores"], n + 1)
                    if n >= 3:
                        dve.wait_ge(na["turned"], n - 2)
                    for r in range(2):
                        b = at["bias"][:, n, 2 - 2 * r:6 - 2 * r, :].rearrange("p j k -> p (j k)")
                        e = V.scalar_tensor_tensor(out=at["s"][:, n % 3, r, :],
                                                   in0=bank[4 + n % 2][:, r * SEQ:(r + 1) * SEQ],
                                                   scalar=0.25 * HD ** -0.5, in1=b, op0=ALU.mult, op1=ALU.add)
                    link(e)
                    link(V.tensor_reduce(at["mx"][:, n % 3, :], at["s"][:, n % 3], AXX, ALU.max))
                    V.tensor_scalar(at["mx"][:, n % 3, :], at["mx"][:, n % 3, :], -1.0, None,
                                    ALU.mult).then_inc(na["biased"], 1)
                n = t - 1
                if 0 <= n < NH:
                    dve.wait_ge(na["exp"], n + 1)
                    link(V.reciprocal(at["rs"][:, n % 3, :], at["sm"][:, n % 3, :]))
                    for r in range(2):
                        e = V.tensor_scalar(at["s"][:, n % 3, r, :], at["s"][:, n % 3, r, :],
                                            at["rs"][:, n % 3, r:r + 1], None, ALU.mult)
                    e.then_inc(na["p"], 1)
                n = t - 5
                if 0 <= n < NH and n % 2:
                    dve.wait_ge(na["out"], n + 1)
                    y_from_bank(at, n // 2, bank[2 + n // 2 % 2][:, 0:SEQ], A, YBASE["in1"])

        def hyena():
            ph = PH["in2"]
            link(V.memset(hy["rawz"][:], 0.0))

            def taps(j, m):
                rz, z = hy["rawz"][:, j % 2], hy["z"][:, m, :]
                col = [vec[:, bass.ds(VEC["c_conv"] + t * 24 + m, 1)] for t in range(3)]
                link(V.tensor_scalar(z, rz[:, 0:SEQ], col[0], v("c_bias", m), ALU.mult, ALU.add))
                for t in (1, 2):
                    link(V.scalar_tensor_tensor(out=z, in0=rz[:, t:t + SEQ], scalar=col[t], in1=z, op0=ALU.mult,
                                                op1=ALU.add))
            dve_steps(ph, 0, 24, scaled(ph, 0, 24, lambda j, m: hy["rawz"][:, j % 2, 1:SEQ + 1], taps), link, 12)
            for n in range(4):
                half, order = n // 2, n % 2
                dve.wait_ge(hs["F"], n + 1)
                fr = hy["frY"]
                for d in range(2):
                    for r in range(2):
                        e = V.tensor_tensor(fr[:, 2 * d + r, :], bank[4 + 2 * d + r][:], hy["decay"][:, r, :], ALU.mult)
                e.then_inc(hs["fr"], 1)
                dve.wait_ge(hs["fr"], n + 1)
                for part, op in enumerate((ALU.add, ALU.subtract)):
                    e = V.tensor_tensor(hy["ab"][:, part], fr[:, 0:2, :], fr[:, 2:4, :], op)
                e.then_inc(hs["ab"], 1)
                dve.wait_ge(hs["abs"], n + 1)
                link(V.tensor_tensor(hy["am"][:], hy["H"][:, 0:2, :], hy["H"][:, 2:4, :], ALU.max))
                V.tensor_copy(hy["am"][0:1, 0, :], hy["H"][0:1, 0, :]).then_inc(hs["am"], 1)
                dve.wait_ge(hs["norm"], n + 1)
                V.reciprocal(hy["inv"][:], bank[0][:, 0:HJ]).then_inc(hs["inv"], 1)
                dve.wait_ge(hs["H"], 5 * n + 5)
                link(V.memset(hy["H"][0:1, 2, :], 0.0))
                dve.wait_ge(hs["U"], n + 1)
                for f in range(2):
                    ur, us = bank[4 + f][:], bank[6 + f][:]
                    H, Yv = hy["H"], hy["frY"]
                    hc, hsn, hx = H[:, f, :], H[:, 2 + f, :], H[:, 4 if f == 0 else 1, :]
                    V.tensor_tensor(Yv[:, f, :], ur, hc, ALU.mult)
                    link(V.tensor_tensor(hy["t1"][:], us, hsn, ALU.mult))
                    link(V.tensor_tensor(Yv[:, f, :], Yv[:, f, :], hy["t1"][:], ALU.subtract))
                    V.tensor_tensor(Yv[:, 2 + f, :], us, hx, ALU.mult)
                    link(V.tensor_tensor(hy["t1"][:], ur, hsn, ALU.mult))
                    e = V.tensor_tensor(Yv[:, 2 + f, :], Yv[:, 2 + f, :], hy["t1"][:], ALU.add)
                    if f == 0:
                        link(e)
                e.then_inc(hs["Y"], 1)
                for j in range(HJ):
                    cc = half * HJ + j
                    t = up[:, j % 2, 0:SEQ]
                    z = hy["z"]
                    link(V.tensor_scalar(t, z[:, cc, :], v("c_skip", order * C + cc), None, ALU.mult))
                    dve.wait_ge(hs["back"], 4 * n + j + 1)
                    link(V.scalar_tensor_tensor(out=t, in0=bank[j][:, 0:SEQ], scalar=hy["inv"][:, j:j + 1], in1=t,
                                                op0=ALU.mult, op1=ALU.add))
                    dst = z[:, cc, :] if order == 0 else hid[:, j % 2, 0:SEQ]
                    V.tensor_tensor(dst, z[:, 8 * (order + 1) + cc, :], t, ALU.mult).then_inc(hs["z"], 1)
                    dve.wait_ge(hs["z"], 4 * n + j + 1)
                    if order:
                        y_from_bank(hy, cc, dst, A, YBASE["in2"])

        def retention():
            ph = PH["in_ret"]
            dve_steps(ph, 0, 24, scaled(ph, 0, 24, lambda j, m: rt["t"][:, m, :]))
            dve.wait_ge(re["loaded"], 32)
            cos, sin = (rt["tab"][:, RTAB[s]:RTAB[s] + L] for s in ("cos", "sin"))
            for i in range(8):
                dve.wait_ge(re["rot"], i + 1)
                t = rt["t"][:, i, :]
                V.tensor_tensor(t, t, cos, ALU.mult)
                link(V.tensor_tensor(up[:, 0, :], bank[4 + i % 2][:, B], sin, ALU.mult))
                V.tensor_tensor(t, t, up[:, 0, :], ALU.add).then_inc(re["roped"], 1)
                dve.wait_ge(re["roped"], i + 1)
            dve.wait_ge(re["lg"], 1)
            V.tensor_scalar(rt["lg"][:], rt["lg"][:], -1.0, None, ALU.mult).then_inc(re["lg"], 1)
            for t in range(RH + 4):
                h = t
                if h < RH:
                    dve.wait_ge(re["scores"], h + 1)
                    dve.wait_ge(re["d"], h + 1)
                    if h >= 2:
                        dve.wait_ge(re["yps"], h - 1)
                    for r, (t0, tn) in enumerate(JT):
                        e = V.scalar_tensor_tensor(out=rt["sd"][0:tn, h % 2, r, :], in0=bank[r][0:tn, B],
                                                   scalar=RDK ** -0.5, in1=rt["e1"][0:tn, h % 2, r, :],
                                                   op0=ALU.mult, op1=ALU.mult)
                    e.then_inc(re["sd"], 1)
                h = t - 3
                if 0 <= h < RH:
                    dve.wait_ge(re["rr"], h + 1)
                    if h == 0:
                        dve.wait_ge(re["silu"], 8)
                    V.tensor_tensor(up[:, 1, :], bank[4 + h % 2][:, B], rt["rr"][:], ALU.mult)\
                        .then_inc(y_ready, 1)
                    dve.wait_ge(y_ready, YR["ret"] + h + 1)
                    link(V.scalar_tensor_tensor(out=hid[:, h % 2, :], in0=up[:, 1, :], scalar=v("gn_w", h),
                                                in1=rt["t"][:, 16 + h, :], op0=ALU.mult, op1=ALU.mult))
                    y_from_bank(rt, h, hid[:, h % 2, :], B, YBASE["ret"])

        def latent():
            ph = PH["in_mla"]
            dve_steps(ph, 0, 6, scaled(ph, 0, 6, lambda j, m: ml["c"][:, m, :]))
            dve.wait_ge(ms["loaded"], 64)
            for g, (c0, cn, gain) in enumerate(((0, QR // P, "q_norm"), (QR // P, KR // P, "kv_norm"))):
                dve.wait_ge(ms["rr"], g + 1)
                rr = ml["rr"][:, g, :]
                link(V.tensor_scalar(ml["ms"][:], bank[4 + g][:, B], 1.0 / (cn * P), EPS, ALU.mult, ALU.add))
                link(V.tensor_tensor(ml["nw"][:], rr, rr, ALU.mult))
                link(V.tensor_tensor(ml["nw"][:], ml["nw"][:], ml["ms"][:], ALU.mult))
                link(V.tensor_scalar(ml["nw"][:], ml["nw"][:], -0.5, 1.5, ALU.mult, ALU.add))
                link(V.tensor_tensor(rr, rr, ml["nw"][:], ALU.mult))
                for i in range(cn):
                    c = ml["c"][:, c0 + i, :]
                    e = V.scalar_tensor_tensor(out=c, in0=c, scalar=v(gain, i), in1=ml["rr"][:, g, :], op0=ALU.mult,
                                               op1=ALU.mult)
                e.then_inc(ms["normed"], 1)
            cos, sin = (ml["tab"][0:MQK, MTAB[s]:MTAB[s] + L] for s in ("cos", "sin"))
            rope = slice(NOPE, MQK)
            dve.wait_ge(ms["krot"], 1)
            V.tensor_tensor(ml["kr"][rope, :], ml["c"][rope, 5, :], cos[rope, :], ALU.mult)
            link(V.tensor_tensor(up[rope, 0, :], bank[6][rope, B], sin[rope, :], ALU.mult))
            V.tensor_tensor(ml["kr"][rope, :], ml["kr"][rope, :], up[rope, 0, :], ALU.add).then_inc(ms["kr"], 1)
            for t in range(MH + 4):
                h = t - 4
                if 0 <= h < MH and h % 2:
                    dve.wait_ge(ms["out"], h + 1)
                    y_from_bank(ml, h // 2, bank[2][:, B], B, YBASE["mla"])
                h = t - 2
                if 0 <= h < MH:
                    dve.wait_ge(ms["exp"], h + 1)
                    for r, tn in ((0, P), (2, JT[2][1])):
                        s = slice(0, 2) if r == 0 else slice(2, 3)
                        link(V.reciprocal(ml["rs"][0:tn, h % 2, s], ml["sm"][0:tn, h % 2, s]))
                    for r, (t0, tn) in enumerate(JT):
                        s = ml["s"][0:tn, h % 2, r, :]
                        e = V.tensor_scalar(s, s, ml["rs"][0:tn, h % 2, r:r + 1], None, ALU.mult)
                    e.then_inc(ms["p"], 1)
                h = t
                if h < MH:
                    q = ml["q"][0:MQK, h % 2, :]
                    dve.wait_ge(ms["qraw"], h + 1)
                    if h >= 2:
                        dve.wait_ge(ms["scores"], h - 1)
                    V.tensor_tensor(q, ml["qraw"][0:MQK, :], cos, ALU.mult)
                    dve.wait_ge(ms["rot"], h + 1)
                    link(V.tensor_tensor(up[0:MQK, 0, :], bank[1][0:MQK, B], sin, ALU.mult))
                    V.tensor_tensor(q, q, up[0:MQK, 0, :], ALU.add).then_inc(ms["q"], 1)
                h = t - 1
                if 0 <= h < MH:
                    dve.wait_ge(ms["scores"], h + 1)
                    for r, (t0, tn) in enumerate(JT):
                        e = V.tensor_reduce(ml["mx"][0:tn, h % 2, r:r + 1], bank[3 + r][0:tn, B], AXX, ALU.max)
                    link(e)
                    V.tensor_scalar(ml["mx"][:, h % 2, 0:2], ml["mx"][:, h % 2, 0:2], -MQK ** -0.5, None, ALU.mult)
                    V.tensor_scalar(ml["mx"][0:JT[2][1], h % 2, 2:3], ml["mx"][0:JT[2][1], h % 2, 2:3], -MQK ** -0.5,
                                    None, ALU.mult).then_inc(ms["max"], 1)

        V.memset(eps[:, 0:1], EPS)
        V.memset(eps[:, 1:2], GN_EPS).then_inc(eps_set, 1)
        V.memset(gate[:, 0, 0:2], 0.0).then_inc(bank_free, 4)
        dve.wait_ge(start_loaded, 64)
        for m in range(C):
            x_parts(m, v("mix_g", m), A, 0)
        for layer, bias in enumerate(("f_b1", "f_b2")):
            dve.wait_ge(filt_ps, layer + 1)
            if layer == 0:
                pass
            F_, S_ = slice(0, FHID), slice(0, SEQ)
            arg, turns, r = up[F_, 0, S_], up[F_, 1, S_], filt_x[:]
            link(V.tensor_scalar(arg, bank[7][F_, S_], v(bias)[F_, :], v("f_freq")[F_, :], ALU.add, ALU.mult))
            link(V.tensor_scalar(turns, arg, 1 / (2 * math.pi), ROUND, ALU.mult, ALU.add))
            link(V.tensor_scalar(turns, turns, -ROUND, None, ALU.add))
            link(V.scalar_tensor_tensor(out=arg, in0=turns, scalar=-TWO_PI_HI, in1=arg, op0=ALU.mult, op1=ALU.add))
            link(V.scalar_tensor_tensor(out=arg, in0=turns, scalar=-TWO_PI_LO, in1=arg, op0=ALU.mult, op1=ALU.add))
            V.tensor_scalar(r, arg, PI_IN, -PI_IN, ALU.min, ALU.max).then_inc(filt_arg, 1)
            if layer == 0:
                for p in range(RING - 1):
                    dve.wait_ge(panel_hi, p + 1)
                    V.tensor_tensor(wlo[:, p, 0:K8 * P], raw[:, p, 0:K8 * P], whi[:, p, 0:K8 * P].bitcast(F32),
                                    ALU.subtract).then_inc(panel_lo, 1)
        norm = 0
        for layer, kind in enumerate(KINDS):
            norm_inv(norm, A)
            norm += 1
            if kind == "conv":
                short_conv(layer)
            elif kind == "attention":
                attention()
            else:
                hyena()
            residual(PH[f"out{layer}"], ("ffn_g", layer * C), A, norm, A)
            norm_inv(norm, A)
            norm += 1
            feed_forward(PH[f"up{layer}"], layer, A)
            last = layer == DEPTH - 1
            residual(PH[f"down{layer}"], ("mix_w2", 0) if last else ("mix_g", (layer + 1) * C), A, norm,
                     B if last else A)
        norm_inv(norm, B)
        norm += 1
        retention()
        latent()
        ph_gate = PH["in_gate"]
        dve_steps(ph_gate, 0, 16, scaled(ph_gate, 0, 16, lambda j, m: mg["g"][:, m, :]))
        ph_ro = PH["ret_out"]
        dve.wait_ge(gate_on, 16)

        def ret_step(i, j, k):
            m = j + 4 * i
            dve.wait_ge(panel_used, ph_ro.p0 + j + 1 + 4 * i)
            V.tensor_tensor(mg["r"][:, m, :], bank[(ph_ro.b0 + j) % 4][:, B], mg["g"][:, m, :],
                            ALU.mult).then_inc(bank_free, 1)
            split_lo(ph_ro, 0, i, j, k)
        dve_steps(ph_ro, 0, 8, ret_step)
        ph_mo = PH["mla_out"]
        for j in range(4):
            dve.wait_ge(panel_used, ph_mo.p0 + j + 1)
            for u in range(2):
                m = 2 * j + u
                V.tensor_tensor(up[:, u, :], bank[(ph_mo.b0 + m) % 4][:, B], mg["g"][:, 8 + m, :],
                                ALU.mult).then_inc(bank_free, 1)
                dve.wait_ge(bank_free, ph_mo.t0 + m + 5)
                V.tensor_tensor(hid[:, u, :], up[:, u, :], mg["r"][:, m, :], ALU.add).then_inc(y_ready, 1)
            split_lo(ph_mo, 0, 0, j, K8)
            for u in range(2):
                m = 2 * j + u
                dve.wait_ge(y_hi, YBASE["mrg"] + m + 1)
                V.tensor_tensor(mg["yl2"][:, m, :], hid[:, u, :], mg["yh2"][:, m, :].bitcast(F32),
                                ALU.subtract).then_inc(y_lo, 1)
        residual(PH["w_o"], ("ffn_w2", 0), B, norm, B)
        norm_inv(norm, B)
        norm += 1
        feed_forward(PH["up4"], DEPTH, B)
        residual(PH["down4"], None, B, norm, B)
        norm_inv(norm, B)
        for m in range(C):
            V.scalar_tensor_tensor(out=x[:, m, A], in0=x[:, m, A], scalar=v("final_w", m), in1=rinv[:, A],
                                   op0=ALU.mult, op1=ALU.mult).then_inc(out_ready, 1)

    ctx.close()


def shape_constants():
    f = np.float32
    con = np.zeros((P, NCON), f)
    con[:, CON["ident"]:CON["ident"] + P] = np.eye(P)
    con[:, CON["ones"]:CON["ones"] + P] = 1
    i = np.arange(P)
    con[:, CON["pair_ones"]:CON["pair_ones"] + P] = i[:, None] // HD == i[None] // HD
    qc, kc = i % GW, np.arange(GW)
    c0 = np.clip(qc - 8, 0, GW - 16)[:, None]
    con[:, CON["colmask"]:CON["colmask"] + GW] = np.where((kc >= c0) & (kc < c0 + 16), 0, -1e30)

    def rope(rows, half, first):
        inv = (f(10000.0) ** (-np.arange(half, dtype=f) / f(half))).astype(f)
        ang = (np.arange(L, dtype=f)[:, None] * inv[None]).astype(f)
        cos, sin, rot = np.ones((P, L), f), np.zeros((P, L), f), np.zeros((P, P), f)
        for r in range(first, rows):
            d = (r - first) % (2 * half)
            cos[r], sin[r] = np.cos(ang[:, d % half]), np.sin(ang[:, d % half])
            if d < half:
                rot[r + half, r] = -1
            else:
                rot[r - half, r] = 1
        return rot, cos, sin

    ret = np.zeros((P, NRTAB), f)
    ret[:, 0:P] = np.eye(P) - 1.0 / P
    rot, cos, sin = rope(P, RDK // 2, 0)
    ret[:, RTAB["rot"]:RTAB["rot"] + P] = rot
    ret[:, RTAB["cos"]:RTAB["cos"] + L] = cos
    ret[:, RTAB["sin"]:RTAB["sin"] + L] = sin
    for r in range(3):
        j, q = r * P + i[:, None], np.arange(L)[None]
        ret[:, RTAB["back"] + r * L:RTAB["back"] + (r + 1) * L] = np.maximum(q - j, 0)
        ret[:, RTAB["ahead"] + r * L:RTAB["ahead"] + (r + 1) * L] = np.maximum(j - q, 0)
    mla = np.zeros((P, NMTAB), f)
    rot, cos, sin = rope(MQK, ROPE // 2, NOPE)
    mla[:, 0:P], mla[:, P:P + L], mla[:, P + L:] = rot, cos, sin

    t = np.arange(SEQ, dtype=np.float64)
    w = 2 * np.pi * np.outer(t, t) / NFFT
    alt = np.where(np.arange(SEQ) % 2, -1.0, 1.0)
    fcos, fsin = np.cos(w), np.sin(w)
    fsin[:, 0] = alt
    last = fcos[:, 0:P].copy()
    last[:, 0] = alt
    fdft = np.concatenate([fcos, fsin, last], 1).astype(f).reshape(2, P, -1).transpose(1, 0, 2)
    icos, isin = 2 * np.cos(w) / NFFT, 2 * np.sin(w) / NFFT
    icos[0] = 1 / NFFT
    isin[0] = alt / NFFT
    idft = np.concatenate([icos, isin], 0).astype(f).reshape(4, P, SEQ).transpose(1, 0, 2)

    tt = np.linspace(0.0, 1.0, SEQ, dtype=f)
    bands = np.linspace(1e-4, 15, 16, dtype=f)
    ang = (f(2.0 * math.pi) * np.arange(SEQ, dtype=f)[:, None] / f(SEQ) * bands).astype(f)
    z = np.concatenate([tt[:, None], np.cos(ang), -np.sin(ang)], -1).astype(f)
    lt = math.log(1e-2)
    deltas = np.abs(np.linspace(lt / 1.5, lt / 0.3, D, dtype=f))
    decay = np.exp(-tt[:, None] * deltas).astype(f).reshape(2, P, D).transpose(1, 0, 2)
    return con, ret, mla, fdft, idft, z.T, decay


def lay_out(w):
    cols = lambda t: t.reshape(-1, P).T

    def tiles(m, starts=None):
        k = m.shape[0] // P
        if starts is None:
            starts = range(0, m.shape[1], P)
        r = m.reshape(k, P, m.shape[1])
        return [np.ascontiguousarray(r[:, :, s:s + P].transpose(1, 0, 2)) for s in starts]

    w8, w11 = [], []

    def add(ts):
        w8.extend(t.reshape(P, -1) for t in ts)

    def add_ffn(g, u, down):
        for p, q in zip(tiles(g), tiles(u)):
            add([p, q])
        for t in tiles(down):
            w11.extend([t[:, :K11].reshape(P, -1), t[:, K11:].reshape(P, -1)])

    mix_in = [w["a_w_in"][0], w["b_w_qkv"][0], w["c_w_in"][0], w["a_w_in"][1]]
    mix_out = [w["a_w_out"][0], w["b_w_out"][0], w["c_w_out"][0], w["a_w_out"][1]]
    for layer in range(DEPTH):
        ts = tiles(mix_in[layer])
        if KINDS[layer] == "conv":
            ts = ts[8:24] + ts[0:8]
        add(ts)
        add(tiles(mix_out[layer]))
        add_ffn(w["f_w13"][layer][:, :FF], w["f_w13"][layer][:, FF:], w["f_w2"][layer])
    wi = w["w_in_2"][0]
    add(tiles(wi, range(0, 3072, P)))
    add(tiles(wi, [3072, 3200, 3328, 3456, 3584, 3712 - NOPE]))
    add(tiles(wi, range(3744, 5792, P)))
    add(tiles(w["w_ret_out_2"][0]))
    mo = tiles(w["w_mla_out_2"][0])
    add([np.concatenate([mo[2 * i], mo[2 * i + 1]], 1) for i in range(4)])
    add(tiles(w["w_o_2"][0]))
    add_ffn(w["w_ffn_gate_2"][0], w["w_ffn_up_2"][0], w["w_ffn_down_2"][0])

    pad = lambda t: np.concatenate([t, np.zeros(P - t.shape[0], t.dtype)])[:, None]
    vec = np.concatenate([
        cols(w["norm_mix_g"]), cols(w["norm_ffn_g"]), cols(w["a_conv_w"]), cols(w["c_short_w"]),
        cols(w["c_short_b"]), cols(w["c_f_skip"]), cols(w["norm_mix_w_2"]), cols(w["norm_ffn_w_2"]),
        cols(w["norm_final_w_2"]), cols(w["ret_gn_w_2"]), cols(w["mla_q_norm_w_2"]), cols(w["mla_kv_norm_w_2"]),
        np.tile(w["b_q_norm_g"][0], 2)[:, None], np.tile(w["b_k_norm_g"][0], 2)[:, None],
        pad(w["c_f_b1"][0]), pad(w["c_f_b2"][0]), pad(w["c_f_freq"][0])], 1)
    con, ret_tab, mla_tab, fdft, idft, zT, decay = shape_constants()
    u, c = np.arange(P)[:, None, None] // GW, np.arange(P)[:, None, None] % GW
    j, k = np.arange(6)[None, :, None], np.arange(GW)[None, None, :]
    bias = w["b_rpb"][0][:, 5 - u + j, np.clip(k - c + 15, 0, 30)].transpose(1, 0, 2, 3)
    chunked = lambda t: t.reshape(-1, P, t.shape[-1]).transpose(1, 0, 2)
    return {
        "xT": chunked(w["x"][0].T), "metaT": chunked(w["meta_tokens_2"].T), "vec": vec, "con": con,
        "w8": np.stack(w8), "w11": np.stack(w11), "bias": bias,
        "filt_in": np.concatenate([zT, w["c_f_w1"][0]], 1), "filt_w2": w["c_f_w2"][0],
        "filt_w3": w["c_f_w3"][0].reshape(FHID, 4, D), "fdft": fdft, "idft": idft, "decay": decay,
        "ret_tab": ret_tab, "mla_tab": mla_tab,
        "decays": np.stack([w["ret_decay_fwd_2"][0], w["ret_decay_bwd_2"][0]])[None],
        "uq": chunked(w["w_uq_2"][0]), "uk": chunked(w["w_uk_2"][0]), "uv": chunked(w["w_uv_2"][0]),
    }


def kernel(**inputs):
    import concourse.bacc as bacc
    from concourse.bass_utils import run_bass_kernel_spmd

    arrays = {n: np.ascontiguousarray(t) for n, t in lay_out({k: np.asarray(t) for k, t in inputs.items()}).items()}
    nc = bacc.Bacc("TRN2", target_bir_lowering=False, num_devices=1)
    args = {n: nc.dram_tensor(f"in_{n}", t.shape, mybir.dt.from_np(t.dtype), kind="ExternalInput").ap()
            for n, t in arrays.items()}
    out = nc.dram_tensor("out", (P, C, SEQ), F32, kind="ExternalOutput").ap()
    build(nc, args, out)
    got = run_bass_kernel_spmd(nc, [{f"in_{n}": t for n, t in arrays.items()}], core_ids=[0]).results[0]["out"]
    return np.ascontiguousarray(got.transpose(2, 1, 0).reshape(1, SEQ, D))
```

```python
import math
from contextlib import ExitStack

import numpy as np
import concourse.bass as bass
from concourse import mybir

F32 = mybir.dt.float32
F32R = mybir.dt.float32r
ALU = mybir.AluOpType
ACT = mybir.ActivationFunctionType
AXX = mybir.AxisListType.X

P = 128
D = 1024
C = D // P
SEQ, META = 256, 16
L = SEQ + META
FF = 2816
FC = FF // P
DEPTH = 4
K8, K11 = 8, FC // 2
RING = 4
SLOT = K11 * P
EPS = 1e-6
GN_EPS = 1e-5
KINDS = ("conv", "attention", "hyena", "conv")

NH, HD, GW = 16, 64, 64
RH, RDK, RDV = 8, 64, 128
MH, NOPE, ROPE, MDV = 8, 64, 32, 64
MQK = NOPE + ROPE
QR, KR = 384, 256
JT = [(0, 128), (128, 128), (256, 16)]

EMB, FHID, NFFT = 33, 64, 2 * SEQ

VEC = {}


def _vec_layout():
    at = 0
    for name, n in (("mix_g", DEPTH * C), ("ffn_g", DEPTH * C), ("a_conv", 2 * 3 * C), ("c_conv", 3 * 24),
                    ("c_bias", 24), ("c_skip", 2 * C), ("mix_w2", C), ("ffn_w2", C), ("final_w", C), ("gn_w", C),
                    ("q_norm", QR // P), ("kv_norm", KR // P), ("q_g", 1), ("k_g", 1), ("f_b1", 1), ("f_b2", 1),
                    ("f_freq", 1)):
        VEC[name] = at
        at += n
    return at


NVEC = _vec_layout()

CON = {}


def _con_layout():
    at = 0
    for name, n in (("ident", P), ("ones", P), ("pair_ones", P), ("colmask", GW)):
        CON[name] = at
        at += n
    return at


NCON = _con_layout()


class Phase:

    def __init__(self, name, panels, k, panel0, tile0, bank0, tiles, block0):
        self.name, self.n, self.k, self.p0, self.t0, self.b0 = name, panels, k, panel0, tile0, bank0
        self.tiles, self.block0 = tiles, block0


def plan():
    out, p, t, b, at = {}, 0, 0, 0, {K8: 0, K11: 0}
    seq = []
    for layer in range(DEPTH):
        seq += [(f"in{layer}", 24, K8, 24), (f"out{layer}", 8, K8, 8), (f"up{layer}", 2 * FC, K8, 2 * FC),
                (f"down{layer}", 16, K11, 8)]
    seq += [("in_ret", 24, K8, 24), ("in_mla", 6, K8, 6), ("in_gate", 16, K8, 16), ("ret_out", 8, K8, 8),
            ("mla_out", 4, K8, 8), ("w_o", 8, K8, 8), ("up4", 2 * FC, K8, 2 * FC), ("down4", 16, K11, 8)]
    for name, n, k, tiles in seq:
        out[name] = Phase(name, n, k, p, t, b, tiles, at[k])
        p, t, at[k] = p + n, t + tiles, at[k] + n
        b = (b + (2 if k == K11 else tiles)) % 4
    names = [s[0] for s in seq]
    for a, nxt in zip(names, names[1:] + [None]):
        out[a].next_k = out[nxt].k if nxt else None
    return out, names, p


PH, ORDER, PANELS = plan()


RTAB = {"center": 0, "rot": P, "cos": 2 * P, "sin": 2 * P + L, "back": 2 * P + 2 * L, "ahead": 2 * P + 5 * L}
NRTAB = 2 * P + 8 * L
MTAB = {"rot": 0, "cos": P, "sin": P + L}
NMTAB = P + 2 * L

HC = 512
HJ = HC // P
YBASE = {"in0": 0, "in1": 8, "in2": 16, "in3": 24, "ret": 32, "mla": 40, "mrg": 44}
TAPS = {"in0": 0, "in2": 8, "in3": 32}
YR = {"in0": 0, "in3": C, "mrg": 2 * C}
NORMS = 2 * DEPTH + 3
TWO_PI_HI = 6.28125
TWO_PI_LO = 2 * math.pi - TWO_PI_HI
ROUND = 1.5 * 2.0 ** 23
PI_IN = 3.1415925


class Chain:

    def __init__(self, eng, sem):
        self.eng, self.sem, self.n = eng, sem, 0

    def __call__(self, ins):
        self.n = self.n + 1
        ins.then_inc(self.sem, 1)
        self.eng.wait_ge(self.sem, self.n)


def build(nc, a, out):
    ctx = ExitStack()

    def sem(name):
        return ctx.enter_context(nc.semaphore(name))

    def sb(name, shape, dt=F32):
        return ctx.enter_context(nc.sbuf_tensor(name, shape, dt))

    def overlay(scope, parts):
        got = {}
        with ExitStack() as stage:
            for name, shape, dt in parts:
                got[name] = stage.enter_context(nc.sbuf_tensor(f"{scope}_{name}", shape, dt))
        return got

    raw = sb("raw", [P, RING, SLOT])
    whi = sb("whi", [P, RING, SLOT], F32R)
    wlo = sb("wlo", [P, RING, SLOT], F32R)
    x = sb("x", [P, C, L])
    hyx = overlay("hyx", [("ab", [P, 2, 2, HC], F32), ("ut", [P, 2, HC], F32), ("am", [P, 2, HC], F32)])
    mlx = overlay("mlx", [("s", [P, 3, 3, L], F32), ("pt", [P, 2, 3, L], F32)])
    xh = sb("xh", [P, C, L], F32R)
    xl = sb("xl", [P, C, L], F32R)
    vec = sb("vec", [P, NVEC])
    con = sb("con", [P, NCON])
    eps = sb("eps", [P, 2])
    sumsq = sb("sumsq", [P, L])
    square = sb("square", [P, L])
    root = sb("root", [P, L])
    rinv = sb("rinv", [P, L])
    mean_sq = sb("mean_sq", [P, L])
    newton = sb("newton", [P, L])
    gate = sb("gate", [P, 2, L])
    silu = sb("silu", [P, 2, L])
    up = sb("up", [P, 2, L])
    hid = sb("hid", [P, 2, L])
    filt_hid = sb("filt_hid", [FHID, SEQ])
    bank = [ctx.enter_context(nc.psum_tensor(f"bank{i}", [P, 512], F32)) for i in range(8)]

    start = overlay("start", [("conv", [P, 40 * 256], F32), ("filt_in", [EMB, SEQ + FHID], F32),
                              ("filt_w2", [FHID, FHID], F32), ("filt_x", [FHID, SEQ], F32)])
    filt_in, filt_w2, filt_x = start["filt_in"], start["filt_w2"], start["filt_x"]
    ffn = overlay("ffn", [("hh", [P, FC, L], F32R), ("hl", [P, FC, L], F32R)])
    Y = [("yh", [P, C, L], F32R), ("yl", [P, C, L], F32R)]
    cm = overlay("conv", Y + [("c", [P, C, SEQ], F32), ("cv", [P, C, SEQ], F32), ("cu", [P, 2, SEQ + 2], F32)])
    att_fixed = [("qkv", [P, 24, SEQ], F32), ("bias", [P, NH, 6, GW], F32), ("nw", [P, 2, 4, SEQ], F32),
                 ("sq", [P, 2, SEQ], F32)]
    at = overlay("att", Y + att_fixed + [("s", [P, 3, 2, SEQ], F32), ("pt", [P, 2, 2, SEQ], F32),
                                         ("vt", [P, 2, 2, P], F32), ("mx", [P, 3, 2], F32), ("sm", [P, 3, 2], F32),
                                         ("rs", [P, 3, 2], F32)])
    an = overlay("att_norm", [("ms", [P, 16, SEQ], F32), ("gap", [P, 2 * C * L - 16 * SEQ], F32)] +
                 att_fixed + [("rr", [P, 16, SEQ], F32)])
    hy = overlay("hy", Y + [("z", [P, 24, SEQ], F32), ("rawz", [P, 2, SEQ + 2], F32),
                            ("H", [P, 2, 5, HC], F32), ("frY", [P, 4, HC], F32), ("t1", [P, HC], F32),
                            ("fdft", [P, 2, 2 * SEQ + P], F32), ("idft", [P, 4, SEQ], F32),
                            ("decay", [P, 2, HC], F32), ("w3", [FHID, 2, HC], F32), ("inv", [P, 2, HJ], F32)]) | hyx
    rt = overlay("ret", Y + [("t", [P, 24, L], F32), ("yc", [P, RH, L], F32), ("var", [P, RH, L], F32),
                             ("vt", [P, 3, D], F32), ("e1", [P, 2, 3, L], F32), ("e2", [P, 3, L], F32),
                             ("sd", [P, 2, 3, L], F32), ("tab", [P, NRTAB], F32),
                             ("dec", [P, 2, RH], F32), ("lg", [P, 2, RH], F32)])
    ML0 = [("retyh", [P, C, L], F32R), ("retyl", [P, C, L], F32R), ("yh", [P, 4, L], F32R), ("yl", [P, 4, L], F32R)]
    ml_early = [("c", [P, 6, L], F32), ("q", [P, 2, L], F32), ("qraw", [P, L], F32), ("k", [P, 2, L], F32),
                ("kr", [P, L], F32), ("vt", [P, 3, MH * MDV], F32), ("sq", [P, 3, L], F32), ("rr", [P, 2, L], F32),
                ("ms", [P, L], F32), ("nw", [P, L], F32), ("mx", [P, 3, 3], F32), ("sm", [P, 3, 3], F32),
                ("rs", [P, 3, 3], F32)]
    ml_used = sum(int(np.prod(sh[1:])) for _, sh, _ in ml_early) + 8 * L
    ml = overlay("mla", ML0 + ml_early + [("gap", [P, max(40 * L - ml_used, 8)], F32),
                                          ("uq", [P, 3, MH * MQK], F32), ("uk", [P, 2, MH * NOPE], F32),
                                          ("uv", [P, 2, MH * MDV], F32), ("tab", [P, NMTAB], F32),
                                          ("g", [P, 16, L], F32)]) | mlx
    def filter_parts(n):
        return [hy["H"][:, 1, 2 * p:2 * p + 2, :] if n == 0 else hy["ab"][:, p] for p in range(2)]

    def magnitudes(n):
        return hy["frY"][:, 0:2, :] if n == 0 else hy["am"][:]

    def sum_bank(n):
        return bank[0 if n else 7]

    def spectrum_bank(n, i):
        return bank[1 + i % 3 if n else 4 + i % 3]

    mg = overlay("mrg", ML0 + [("r", [P, C, L], F32)] +
                 [("yh2", [P, C, L], F32R), ("yl2", [P, C, L], F32R)])

    def v(name, m=0):
        return vec[:, bass.ds(VEC[name] + m, 1)]

    def k_(name, n, rows=P):
        return con[0:rows, CON[name]:CON[name] + n]

    ident, ones = k_("ident", P), k_("ones", P)
    A = slice(META, L)
    B = slice(0, L)

    loaded = [sem(f"panel_loaded{i}") for i in range(RING)]
    start_loaded = sem("start_loaded")
    filt_loaded = sem("filt_loaded")
    panel_hi, panel_lo, panel_used = sem("panel_hi"), sem("panel_lo"), sem("panel_used")
    bank_free = sem("proj_bank_free")
    x_hi, x_lo = sem("x_hi"), sem("x_lo")
    sumsq_done, norm_total, root_ready, rinv_ready = (sem("sumsq_done"), sem("norm_total"), sem("root_ready"),
                                                      sem("rinv_ready"))
    gate_silu, hid_ready, hid_hi, hid_lo = sem("gate_silu"), sem("hid_ready"), sem("hid_hi"), sem("hid_lo")
    y_ready, y_hi, y_lo = sem("y_ready"), sem("y_hi"), sem("y_lo")
    dve_chain, act_chain, pool_chain = sem("dve_chain"), sem("act_chain"), sem("pool_chain")
    eps_set = sem("eps_set")
    filt_ps, filt_arg, filt_sin = sem("filt_ps"), sem("filt_arg"), sem("filt_sin")
    bias_loaded, bias_masked = sem("bias_loaded"), sem("bias_masked")
    na = {s: sem(f"na_{s}") for s in ("near_one", "squared", "sums", "ms", "rr", "rr2", "newton", "vps", "vt", "qk",
                                      "scores",
                                      "biased", "exp", "p", "turned", "pt", "out")}
    hs = {s: sem(f"hy_{s}") for s in ("tables", "filter_in", "F", "fr", "ab", "abs", "am", "norm", "inv", "Hps", "H",
                                      "turned", "ut", "U", "Y", "back", "z")}
    re = {s: sem(f"ret_{s}") for s in ("loaded", "lg", "silu", "rot", "roped", "vps", "vt", "e", "d", "scores", "sd",
                                       "yps", "y", "centred", "yc", "squared", "vps2", "var", "rr")}
    ms = {s: sem(f"mla_{s}") for s in ("loaded", "squared", "sums", "rr", "normed", "krot", "kr", "vps", "vt", "pt1",
                                       "qps", "qraw", "rot", "q", "kps", "k", "scores", "max", "exp", "p",
                                       "turned", "pt0", "pt", "out")}
    gate_on = sem("gate_on")
    first_squares = sem("first_squares")
    conv_in, first_tap = sem("conv_in"), sem("first_tap")
    out_ready, stored = sem("out_ready"), sem("stored")

    block = ctx.enter_context(nc.Block())

    def tiles_out(ph):
        return ph.t0 + ph.tiles + 4

    @block.sync
    def _(sp):
        sp.dma_start(x[:, :, A], a["xT"]).then_inc(start_loaded, 16)
        sp.dma_start(x[:, :, 0:META], a["metaT"]).then_inc(start_loaded, 16)
        sp.dma_start(vec[:], a["vec"]).then_inc(start_loaded, 16)
        sp.dma_start(con[:], a["con"]).then_inc(start_loaded, 16)
        sp.dma_start(filt_in[:], a["filt_in"]).then_inc(filt_loaded, 16)
        sp.dma_start(filt_w2[:], a["filt_w2"]).then_inc(filt_loaded, 16)

        def panels(ph, first, n):
            src, width = (a["w8"], K8 * P) if ph.k == K8 else (a["w11"], K11 * P)

            def one(i, j):
                p = ph.p0 + first + j + 4 * i
                slot = (ph.p0 + first + j) % RING
                if ph.p0 + first >= RING:
                    sp.wait_ge(panel_lo, p - RING + 1)
                sp.dma_start(raw[:, slot, 0:width], src[ph.block0 + first + j + 4 * i]).then_inc(loaded[slot], 16)

            if n >= 8:
                with sp.Fori(0, n // 4) as i:
                    for j in range(4):
                        one(i, j)
                for j in range(n % 4):
                    one(n // 4, j)
            else:
                for j in range(n):
                    one(0, j)

        def filter_inputs(n):
            half, order = n // 2, n % 2
            sp.dma_start(hy["w3"][:], a["filt_w3"][:, 2 * order:2 * order + 2,
                                                  half * HC:(half + 1) * HC]).then_inc(hs["filter_in"], 16)
            sp.dma_start(hy["decay"][:], a["decay"][:, :, half * HC:(half + 1) * HC])\
                .then_inc(hs["filter_in"], 16)

        for name in ORDER:
            ph = PH[name]
            if name == "in0":
                panels(ph, 0, 4)
                panels(ph, 4, 20)
            elif name == "in1":
                panels(ph, 0, 8)
                sp.wait_ge(panel_used, ph.p0)
                sp.dma_start(at["bias"][:], a["bias"]).then_inc(bias_loaded, 16)
                panels(ph, 8, 16)
            elif name == "in2":
                panels(ph, 0, 8)
                sp.wait_ge(panel_used, ph.p0)
                sp.dma_start(hy["fdft"][:], a["fdft"]).then_inc(hs["tables"], 16)
                sp.dma_start(hy["idft"][:], a["idft"]).then_inc(hs["tables"], 16)
                filter_inputs(0)
                panels(ph, 8, 16)
            elif name == "out2":
                panels(ph, 0, 4)
                for n in range(1, 4):
                    sp.wait_ge(hs["fr"], n)
                    filter_inputs(n)
                panels(ph, 4, 4)
            elif name == "in_ret":
                panels(ph, 0, 8)
                sp.wait_ge(panel_used, ph.p0)
                sp.dma_start(rt["tab"][:], a["ret_tab"]).then_inc(re["loaded"], 16)
                sp.dma_start(rt["dec"][:], a["decays"].broadcast_to([P, 2, RH])).then_inc(re["loaded"], 16)
                panels(ph, 8, 16)
            elif name == "in_mla":
                panels(ph, 0, 6)
            elif name == "in_gate":
                panels(ph, 0, 4)
                sp.wait_ge(re["centred"], RH)
                sp.wait_ge(re["sd"], RH)
                sp.dma_start(ml["tab"][:], a["mla_tab"]).then_inc(ms["loaded"], 16)
                sp.dma_start(ml["uq"][:], a["uq"]).then_inc(ms["loaded"], 16)
                sp.dma_start(ml["uk"][:], a["uk"]).then_inc(ms["loaded"], 16)
                sp.dma_start(ml["uv"][:], a["uv"]).then_inc(ms["loaded"], 16)
                panels(ph, 4, 12)
            else:
                panels(ph, 0, ph.n)

        for m in range(C):
            sp.wait_ge(out_ready, m + 1)
            sp.dma_start(out[:, m, :], x[:, m, A]).then_inc(stored, 16)
        sp.wait_ge(stored, 16 * C)

    @block.tensor
    def _(pe):
        def panel(ph, i, j, hi, lo, cols, ready):
            slot = (ph.p0 + j) % RING
            pe.wait_ge(panel_lo, ph.p0 + j + 1 + 4 * i)
            if ph.name == "mla_out":
                groups = [(2 * j, range(4)), (2 * j + 1, range(4))]
            elif ph.k == K11:
                groups = [(j // 2, range(K11 * (j % 2), K11 * (j % 2) + K11))]
            else:
                groups = [(j, range(K8))]
            w = 0
            for tile, ks in groups:
                ps = bank[(ph.b0 + tile) % 4][:, 0:cols.stop - cols.start]
                if ph.k == K11 and j % 2 == 0:
                    pe.wait_ge(bank_free, ph.t0 + tile + 3 + 2 * i)
                elif ph.k == K8:
                    pe.wait_ge(bank_free, ph.t0 + tile + 1 + (8 if ph.name == "mla_out" else 4) * i)
                for k in ks:
                    if ready is not None and (j == 0 or (ph.k == K11 and j == 1)):
                        pe.wait_ge(ready[0], ready[1] + k + 1)
                    wc = slice(w * P, (w + 1) * P)
                    first = k == 0
                    last = k == (FC - 1 if ph.k == K11 else len(ks) - 1)
                    pe.matmul(ps, whi[:, slot, wc], hi[:, k, cols], start=first, stop=False)
                    pe.matmul(ps, whi[:, slot, wc], lo[:, k, cols], start=False, stop=False)
                    mm = pe.matmul(ps, wlo[:, slot, wc], hi[:, k, cols], start=False, stop=last)
                    w += 1
            mm.then_inc(panel_used, 1)

        def total(norm, cols):
            if norm:
                pe.wait_ge(sumsq_done, norm)
                mm = pe.matmul(bank[7][:, cols], ones, sumsq[:, cols], start=True, stop=True)
            else:
                pe.wait_ge(first_squares, 1)
                for k in range(C):
                    mm = pe.matmul(bank[7][:, cols], ones, cm["cv"][:, k, :], start=k == 0, stop=k == C - 1)
            mm.then_inc(norm_total, 1)

        def product(name, hi, lo, cols, ready, norm=None):
            ph = PH[name]
            rounds, first = ph.n // 4, 0
            if norm is not None:
                for j in range(4):
                    panel(ph, 0, j, hi, lo, cols, ready)
                    if j == 0 and norm:
                        total(norm, cols)
                first = 1
            if rounds - first > 1:
                with pe.Fori(first, rounds) as i:
                    for j in range(4):
                        panel(ph, i, j, hi, lo, cols, ready)
            else:
                for i in range(first, rounds):
                    for j in range(4):
                        panel(ph, i, j, hi, lo, cols, ready)
            for j in range(ph.n % 4):
                panel(ph, rounds, j, hi, lo, cols, None)

        def filter_layer(layer):
            if layer == 0:
                pe.wait_ge(filt_loaded, 32)
                w, y = filt_in[:, SEQ:SEQ + FHID], filt_in[:, 0:SEQ]
            else:
                pe.wait_ge(filt_sin, 1)
                w, y = filt_w2[:], filt_hid[:]
            pe.matmul(bank[6][0:FHID, 0:SEQ], w, y, start=True, stop=True).then_inc(filt_ps, 1)

        def attention_in(norm):
            ph = PH["in1"]

            def head_sums(i, j, m):
                pe.wait_ge(na["squared"], m + 1)
                if j >= 2:
                    pe.wait_ge(na["ms"], m - 1)
                elif i is not None:
                    pe.wait_ge(na["ms"], m - 1)
                pe.matmul(bank[4 + j % 2][:, 0:SEQ], k_("pair_ones", P), at["sq"][:, j % 2, :], start=True,
                          stop=True).then_inc(na["sums"], 1)

            for j in range(4):
                panel(ph, 0, j, xh, xl, A, (x_lo, C * norm))
                if j == 0:
                    total(norm, A)
                if j >= 2:
                    head_sums(None, j - 2, j - 2)
            with pe.Fori(1, 4) as i:
                for j in range(4):
                    panel(ph, i, j, xh, xl, A, None)
                    head_sums(i, (j + 2) % 4, 4 * i + j - 2)
            for j in range(4):
                panel(ph, 4, j, xh, xl, A, None)
                if j < 2:
                    head_sums(4, j, 14 + j)
            for j in range(4):
                panel(ph, 5, j, xh, xl, A, None)

        def attention():
            for t in range(NH + 5):
                if t == 2:
                    pe.wait_ge(bank_free, tiles_out(PH["in1"]))
                if t % 2 == 0 and 2 <= t < NH + 2:
                    c = t // 2 - 1
                    if c:
                        pe.wait_ge(na["vt"], c)
                    for r in range(2):
                        mm = pe.transpose(bank[1][:, r * P:(r + 1) * P], at["qkv"][:, 16 + c, r * P:(r + 1) * P], ident)
                    mm.then_inc(na["vps"], 1)
                n = t
                if n < NH:
                    if n == 0:
                        pe.wait_ge(na["qk"], 4)
                    if n >= 2:
                        pe.wait_ge(na["biased"], n - 1)
                    rows = slice(HD * (n % 2), HD * (n % 2) + HD)
                    for r in range(2):
                        mm = pe.matmul(bank[4 + n % 2][:, r * SEQ:(r + 1) * SEQ],
                                       at["qkv"][rows, n // 2, r * P:(r + 1) * P],
                                       at["qkv"][rows, 8 + n // 2, :], start=True, stop=True)
                    mm.then_inc(na["scores"], 1)
                n = t - 2
                if 0 <= n < NH:
                    pe.wait_ge(na["p"], n + 1)
                    if n >= 2:
                        pe.wait_ge(na["pt"], n - 1)
                    for kt in range(2):
                        for r in range(2):
                            mm = pe.transpose(bank[6 + n % 2][:, kt * SEQ + r * P:kt * SEQ + (r + 1) * P],
                                              at["s"][:, n % 3, r, kt * P:(kt + 1) * P], ident)
                    mm.then_inc(na["turned"], 1)
                n = t - 4
                if 0 <= n < NH:
                    c = n // 2
                    pe.wait_ge(na["pt"], n + 1)
                    pe.wait_ge(na["vt"], c + 1)
                    if c >= 2:
                        pe.wait_ge(y_lo, YBASE["in1"] + c - 1)
                    rows = slice(HD * (n % 2), HD * (n % 2) + HD)
                    for kt in range(2):
                        mm = pe.matmul(bank[2 + c % 2][rows, 0:SEQ], at["vt"][:, c % 2, kt, rows],
                                       at["pt"][:, n % 2, kt, :], start=kt == 0, stop=kt == 1)
                    mm.then_inc(na["out"], 1)
            pe.wait_ge(y_lo, YBASE["in1"] + C)

        def hyena(norm):
            def filters(n):
                pe.wait_ge(hs["filter_in"], 32 * (n + 1))
                if n == 1:
                    pe.wait_ge(hs["H"], 5)
                    pe.wait_ge(hs["inv"], 1)
                elif n:
                    pe.wait_ge(hs["Y"], n - 1)
                for d in range(2):
                    for r in range(2):
                        mm = pe.matmul(bank[4 + 2 * d + r][:], filt_hid[:, r * P:(r + 1) * P], hy["w3"][:, d, :],
                                       start=True, stop=True)
                mm.then_inc(hs["F"], 1)

            def filter_sums(n):
                pe.wait_ge(hs["am"], n + 1)
                if n:
                    pe.wait_ge(hs["inv"], n)
                for j in range(HJ):
                    for r in range(2):
                        mm = pe.matmul(sum_bank(n)[:, j:j + 1], magnitudes(n)[:, r, j * P:(j + 1) * P], ones[:, 0:1],
                                       start=r == 0, stop=r == 1)
                mm.then_inc(hs["norm"], 1)

            def filter_spectra(n, rows):
                for i in rows:
                    part, col = ((0, 0), (0, P), (1, SEQ), (1, SEQ + P), (0, 2 * SEQ))[i]
                    if i >= 3:
                        pe.wait_ge(hs["H"], 5 * n + i - 2)
                    for r in range(2):
                        mm = pe.matmul(spectrum_bank(n, i)[:], hy["fdft"][:, r, col:col + P],
                                       filter_parts(n)[part][:, r, :],
                                       start=r == 0, stop=r == 1)
                    mm.then_inc(hs["Hps"], 1)

            ph = PH["in2"]
            for j in range(4):
                panel(ph, 0, j, xh, xl, A, (x_lo, C * norm))
                if j == 0:
                    total(norm, A)
            with pe.Fori(1, 4) as i:
                for j in range(4):
                    panel(ph, i, j, xh, xl, A, None)
            pe.wait_ge(hs["tables"], 32)
            filters(0)
            for j in range(4):
                panel(ph, 4, j, xh, xl, A, None)
            for j, rows in enumerate(((), (0, 1, 2), (3, 4), ())):
                panel(ph, 5, j, xh, xl, A, None)
                if j == 1:
                    filter_sums(0)
                filter_spectra(0, rows)
            filters(1)
            pe.wait_ge(bank_free, tiles_out(PH["in2"]))
            for n in range(4):
                half = n // 2
                if 0 < n < 3:
                    filters(n + 1)
                if n:
                    pe.wait_ge(hs["z"], 4 * n)
                for r in range(2):
                    for j in range(HJ):
                        mm = pe.transpose(bank[3 * r][:, j * P:(j + 1) * P],
                                          hy["z"][:, half * HJ + j, r * P:(r + 1) * P], ident)
                mm.then_inc(hs["turned"], 1)
                pe.wait_ge(hs["ut"], n + 1)
                if n < 3:
                    pe.wait_ge(hs["fr"], n + 2)
                for i, f in enumerate((0, 2, 1, 3)):
                    for r in range(2):
                        mm = pe.matmul(bank[4 + f][:], hy["fdft"][:, r, f * P:(f + 1) * P], hy["ut"][:, r, :],
                                       start=r == 0, stop=r == 1)
                    if i % 2:
                        mm.then_inc(hs["U"], 1)
                if n < 3:
                    filter_sums(n + 1)
                    filter_spectra(n + 1, range(5))
                    pe.wait_ge(hs["inv"], n + 2)
                    pe.wait_ge(hs["H"], 5 * n + 10)
                pe.wait_ge(hs["Y"], n + 1)
                for j in range(HJ):
                    for i in range(4):
                        mm = pe.matmul(bank[j][:, 0:SEQ], hy["frY"][:, i, j * P:(j + 1) * P], hy["idft"][:, i, :],
                                       start=i == 0, stop=i == 3)
                    mm.then_inc(hs["back"], 1)
            pe.wait_ge(y_lo, YBASE["in2"] + C)

        def retention():
            pe.wait_ge(bank_free, tiles_out(PH["in_ret"]))
            pe.wait_ge(re["loaded"], 32)
            rot = rt["tab"][:, RTAB["rot"]:RTAB["rot"] + P]
            centre = rt["tab"][:, RTAB["center"]:RTAB["center"] + P]
            for i in range(8):
                if i >= 2:
                    pe.wait_ge(re["roped"], i - 1)
                pe.matmul(bank[4 + i % 2][:, B], rot, rt["t"][:, i, :], start=True, stop=True).then_inc(re["rot"], 1)
                if i >= 2:
                    pe.wait_ge(re["vt"], i - 1)
                for r, (t0, tn) in enumerate(JT):
                    mm = pe.transpose(bank[6 + i % 2][0:tn, r * P:(r + 1) * P], rt["t"][:, 8 + i, t0:t0 + tn], ident)
                mm.then_inc(re["vps"], 1)
            pe.wait_ge(re["roped"], 8)
            pe.wait_ge(re["vt"], 8)
            for t in range(RH + 6):
                h = t
                if h < RH:
                    rows = slice(RDK * (h % 2), RDK * (h % 2) + RDK)
                    if h:
                        pe.wait_ge(re["sd"], h)
                    for r, (t0, tn) in enumerate(JT):
                        mm = pe.matmul(bank[r][0:tn, B], rt["t"][rows, 4 + h // 2, t0:t0 + tn],
                                       rt["t"][rows, h // 2, :], start=True, stop=True)
                    mm.then_inc(re["scores"], 1)
                h = t - 5
                if 0 <= h < RH:
                    pe.wait_ge(re["squared"], h + 1)
                    if h >= 2:
                        pe.wait_ge(re["var"], h - 1)
                    pe.matmul(bank[6 + h % 2][:, B], ones, gate[:, h % 2, :], start=True,
                              stop=True).then_inc(re["vps2"], 1)
                h = t - 3
                if 0 <= h < RH:
                    pe.wait_ge(re["y"], h + 1)
                    if h:
                        pe.wait_ge(re["yc"], h)
                    pe.matmul(bank[5][:, B], centre, silu[:, h % 2, :], start=True,
                              stop=True).then_inc(re["centred"], 1)
                h = t - 1
                if 0 <= h < RH:
                    pe.wait_ge(re["sd"], h + 1)
                    if h >= 2:
                        pe.wait_ge(re["y"], h - 1)
                    for r, (t0, tn) in enumerate(JT):
                        mm = pe.matmul(bank[3 + h % 2][:, B], rt["vt"][0:tn, r, h * P:(h + 1) * P],
                                       rt["sd"][0:tn, h % 2, r, :], start=r == 0, stop=r == 2)
                    mm.then_inc(re["yps"], 1)
            pe.wait_ge(re["y"], RH)

        def latent():
            rot = ml["tab"][0:MQK, MTAB["rot"]:MTAB["rot"] + MQK]

            def gate_panels(i, js):
                for j in js:
                    panel(PH["in_gate"], i, j, xh, xl, B, None)

            def squares_sum(g, cn):
                pe.wait_ge(ms["squared"], g + 1)
                for i in range(cn):
                    mm = pe.matmul(bank[4 + g][:, B], ones, ml["sq"][:, i, :], start=i == 0, stop=i == cn - 1)
                mm.then_inc(ms["sums"], 1)

            gate_panels(0, range(4))
            gate_panels(1, range(1))
            squares_sum(0, QR // P)
            gate_panels(1, range(1, 2))
            squares_sum(1, KR // P)
            pe.wait_ge(bank_free, tiles_out(PH["in_mla"]))
            pe.wait_ge(ms["loaded"], 64)
            pe.matmul(bank[6][0:MQK, B], rot, ml["c"][0:MQK, 5, :], start=True, stop=True).then_inc(ms["krot"], 1)
            gate_panels(1, range(2, 4))
            with pe.Fori(2, 4) as i:
                gate_panels(i, range(4))
            pe.wait_ge(ms["normed"], 2)
            pe.wait_ge(ms["kr"], 1)
            for r, (t0, tn) in enumerate(JT):
                for i in range(2):
                    mm = pe.matmul(bank[4 + r][0:tn, :], ml["c"][:, 3 + i, t0:t0 + tn], ml["uv"][:, i, :],
                                   start=i == 0, stop=i == 1)
                mm.then_inc(ms["vps"], 1)
            pe.wait_ge(bank_free, tiles_out(PH["in_gate"]))
            pe.wait_ge(ms["vt"], 3)
            for t in range(MH + 4):
                h = t
                if h < MH:
                    if h:
                        pe.wait_ge(ms["k"], h)
                    for i in range(3):
                        mm = pe.matmul(bank[0][0:MQK, B], ml["uq"][:, i, h * MQK:(h + 1) * MQK], ml["c"][:, i, :],
                                       start=i == 0, stop=i == 2)
                    mm.then_inc(ms["qps"], 1)
                    pe.wait_ge(ms["qraw"], h + 1)
                    if h:
                        pe.wait_ge(ms["q"], h)
                    pe.matmul(bank[1][0:MQK, B], rot, ml["qraw"][0:MQK, :], start=True,
                              stop=True).then_inc(ms["rot"], 1)
                    for i in range(2):
                        mm = pe.matmul(bank[0][0:NOPE, B], ml["uk"][:, i, h * NOPE:(h + 1) * NOPE],
                                       ml["c"][:, 3 + i, :], start=i == 0, stop=i == 1)
                    mm.then_inc(ms["kps"], 1)
                h = t - 4
                if 0 <= h < MH:
                    pe.wait_ge(ms["pt1"], h + 1)
                    pe.wait_ge(ms["pt"], h + 1)
                    if h >= 2 and h % 2 == 0:
                        pe.wait_ge(y_lo, YBASE["mla"] + h // 2)
                    rows = slice(MDV * (h % 2), MDV * (h % 2) + MDV)
                    for r, (t0, tn) in enumerate(JT):
                        mm = pe.matmul(bank[2][rows, B], ml["vt"][0:tn, r, h * MDV:(h + 1) * MDV],
                                       ml["pt"][0:tn, h % 2, r, :], start=r == 0, stop=r == 2)
                    mm.then_inc(ms["out"], 1)
                h = t - 1
                if 0 <= h < MH:
                    pe.wait_ge(ms["q"], h + 1)
                    pe.wait_ge(ms["k"], h + 1)
                    if h:
                        pe.wait_ge(ms["exp"], h)
                    for r, (t0, tn) in enumerate(JT):
                        mm = pe.matmul(bank[3 + r][0:tn, B], ml["q"][0:MQK, h % 2, t0:t0 + tn],
                                       ml["k"][0:MQK, h % 2, :], start=True, stop=True)
                    mm.then_inc(ms["scores"], 1)
                h = t - 3
                if 0 <= h < MH:
                    pe.wait_ge(ms["p"], h + 1)
                    for r, (t0, tn) in enumerate(JT):
                        if r == 2:
                            pe.wait_ge(ms["pt0"], h + 1)
                        elif h:
                            pe.wait_ge(ms[("pt", "pt1")[r]], h)
                        for q, (q0, qn) in enumerate(JT):
                            mm = pe.transpose(bank[6 + r % 2][0:tn, q0:q0 + qn], ml["s"][0:qn, h % 3, q, t0:t0 + tn],
                                              k_("ident", P)[0:qn, 0:qn])
                        mm.then_inc(ms["turned"], 1)
            pe.wait_ge(y_lo, YBASE["mla"] + 4)

        pe.wait_ge(start_loaded, 64)
        filter_layer(0)
        total(0, A)
        norm = 0
        for layer, kind in enumerate(KINDS):
            if kind == "attention":
                attention_in(norm)
                attention()
            elif kind == "hyena":
                hyena(norm)
            else:
                product(f"in{layer}", xh, xl, A, (x_lo, C * norm), norm)
            if layer == 0:
                filter_layer(1)
            norm += 1
            bufs = {"conv": cm, "attention": at, "hyena": hy}[kind]
            product(f"out{layer}", bufs["yh"], bufs["yl"], A, (y_lo, YBASE[f"in{layer}"]))
            product(f"up{layer}", xh, xl, A, (x_lo, C * norm), norm)
            norm += 1
            product(f"down{layer}", ffn["hh"], ffn["hl"], A, (hid_lo, FC * layer))
        product("in_ret", xh, xl, B, (x_lo, C * norm), norm)
        norm += 1
        retention()
        product("in_mla", xh, xl, B, None)
        latent()
        product("ret_out", rt["yh"], rt["yl"], B, None)
        product("mla_out", ml["yh"], ml["yl"], B, None)
        product("w_o", mg["yh2"], mg["yl2"], B, (y_lo, YBASE["mrg"]))
        product("up4", xh, xl, B, (x_lo, C * norm), norm)
        norm += 1
        product("down4", ffn["hh"], ffn["hl"], B, (hid_lo, FC * DEPTH))
        pe.wait_ge(sumsq_done, norm)
        pe.matmul(bank[7][:, B], ones, sumsq[:], start=True, stop=True).then_inc(norm_total, 1)
        assert norm + 1 == NORMS

    def steps(eng, ph, first, n, step, chain=None, per=0, ahead=4):
        crossing = first + n == ph.n and ph.next_k != ph.k
        rounds = n // 4 - (1 if crossing else 0)

        def one(i, j, split):
            step(i, j, split)

        if rounds > 1:
            start = chain.n if chain else 0
            with eng.Fori(0, rounds) as i:
                if chain:
                    chain.n = start + i * per
                for j in range(4):
                    one(i, j, ph.k)
            if chain:
                chain.n = start + rounds * per
        else:
            for i in range(rounds):
                for j in range(4):
                    one(i, j, ph.k)
        for i in range(rounds, n // 4):
            for j in range(4):
                one(i, j, ph.next_k if j + ahead >= 4 else ph.k)
        for j in range(n % 4):
            one(n // 4, j, ph.k)

    @block.scalar
    def _(act):
        link = Chain(act, act_chain)

        def split_hi(ph, first, i, j, k):
            if k is None:
                return
            p = ph.p0 + first + j
            act.wait_ge(loaded[p % RING], 16 * (p // RING + 2) + 16 * i)
            act.wait_ge(panel_used, p + 1 + 4 * i)
            nc.scalar.copy(whi[:, p % RING, 0:k * P], raw[:, p % RING, 0:k * P]).then_inc(panel_hi, 1)

        def norm_root(norm, cols):
            act.wait_ge(norm_total, norm + 1)
            nc.scalar.activation(root[:, cols], bank[7][:, cols], ACT.Sqrt, bias=eps[:, 0:1],
                                 scale=1.0 / D).then_inc(root_ready, 1)

        def only_split(ph, first=0, n=None):
            def step(i, j, k):
                split_hi(ph, first, i, j, k)
            steps(act, ph, first, ph.n if n is None else n, step)

        def conv_tap(name, m):
            base = VEC["c_conv"] if name == "in2" else VEC["a_conv"] + (int(name[2:]) // 3) * 3 * C
            return vec[:, bass.ds(base + m, 1)]

        def first_taps(ph, first, n):
            def step(i, j, k):
                m = j + 4 * i
                split_hi(ph, first, i, j, k)
                if ph.name == "in2":
                    act.wait_ge(bank_free, ph.t0 + j + 5 + 4 * i)
                    src, dst, bias = hy["rawz"][:, j % 2, 0:SEQ], hy["z"][:, m, :], v("c_bias", m)
                else:
                    act.wait_ge(conv_in, TAPS[ph.name] - (24 if ph.name == "in3" else 0) + j + 1 + 4 * i)
                    src, dst, bias = cm["cu"][:, j % 2, 0:SEQ], cm["cv"][:, m, :], 0.0
                nc.scalar.activation(dst, src, ACT.Identity, bias=bias,
                                     scale=conv_tap(ph.name, m)).then_inc(first_tap, 1)
            steps(act, ph, first, n, step)
            return step

        def gates(ph, ffn_index, cols):
            w = slice(0, cols.stop - cols.start)
            g0 = ffn_index * FC

            def step(i, j, k):
                s = j // 2
                split_hi(ph, 0, i, j, k)
                if j % 2 == 0:
                    act.wait_ge(bank_free, ph.t0 + j + 5 + 4 * i)
                    nc.scalar.activation(silu[:, s, w], gate[:, s, w], ACT.Silu).then_inc(gate_silu, 1)
                else:
                    act.wait_ge(hid_ready, g0 + s + 1 + 2 * i)
                    nc.scalar.copy(ffn["hh"][:, s + 2 * i, cols], hid[:, s, w]).then_inc(hid_hi, 1)
            steps(act, ph, 0, ph.n, step)

        def y_high(ph, first, n, dst, cols, ready0):
            w = slice(0, cols.stop - cols.start)

            def step(i, j, k):
                split_hi(ph, first, i, j, k)
                act.wait_ge(y_ready, ready0 + j + 1 + 4 * i)
                nc.scalar.copy(dst[:, j + 4 * i, cols], hid[:, j % 2, w]).then_inc(y_hi, 1)
            steps(act, ph, first, n, step)

        def attention():
            ph = PH["in1"]

            def squares(i, j, k):
                m = j + 4 * i
                split_hi(ph, 0, i, j, k)
                act.wait_ge(bank_free, ph.t0 + j + 5 + 4 * i)
                if not (isinstance(i, int) and m < 2):
                    act.wait_ge(na["sums"], m - 1)
                    nc.scalar.activation(an["ms"][:, m - 2, :], bank[4 + j % 2][:, 0:SEQ], ACT.Identity,
                                         bias=eps[:, 0:1], scale=1.0 / HD).then_inc(na["ms"], 1)
                nc.scalar.activation(at["sq"][:, j % 2, :], at["qkv"][:, m, :], ACT.Square).then_inc(na["squared"], 1)

            for j in range(4):
                squares(0, j, K8)
            with act.Fori(1, 4) as i:
                for j in range(4):
                    squares(i, j, K8)
            act.wait_ge(na["ms"], 12)
            link(nc.scalar.activation(an["rr"][:, 0:12, :], an["ms"][:, 0:12, :], ACT.Ln))
            for m in (14, 15):
                act.wait_ge(na["sums"], m + 1)
                nc.scalar.activation(an["ms"][:, m, :], bank[4 + m % 2][:, 0:SEQ], ACT.Identity,
                                     bias=eps[:, 0:1], scale=1.0 / HD).then_inc(na["ms"], 1)

            def split(j):
                split_hi(ph, 16, 0, j, K8)

            split(0)
            act.wait_ge(na["ms"], 16)
            link(nc.scalar.activation(an["rr"][:, 12:16, :], an["ms"][:, 12:16, :], ACT.Ln))
            split(1)
            for g in range(4):
                rr = an["rr"][:, 4 * g:4 * g + 4, :]
                nc.scalar.activation(rr, rr, ACT.Exp, scale=-0.5).then_inc(na["rr"], 1)
                act.wait_ge(na["rr"], g + 1)
                if g >= 2:
                    act.wait_ge(na["newton"], g - 1)
                nc.scalar.activation(an["nw"][:, g % 2], rr, ACT.Square).then_inc(na["rr2"], 1)
                split(2 + g)
            split(6)
            split(7)
            act.wait_ge(na["qk"], 4)
            for t in range(NH + 4):
                n = t - 3
                if 0 <= n < NH:
                    act.wait_ge(na["turned"], n + 1)
                    if n >= 2:
                        act.wait_ge(na["out"], n - 1)
                    nc.scalar.copy(at["pt"][:, n % 2].rearrange("p a b -> p (a b)"),
                                   bank[6 + n % 2][:]).then_inc(na["pt"], 1)
                if t % 2 == 0 and 2 <= t < NH + 2:
                    c = t // 2 - 1
                    act.wait_ge(na["vps"], c + 1)
                    if c >= 2:
                        act.wait_ge(na["out"], 2 * c - 2)
                    nc.scalar.copy(at["vt"][:, c % 2].rearrange("p a b -> p (a b)"),
                                   bank[1][:, 0:2 * P]).then_inc(na["vt"], 1)
                n = t
                if 0 <= n < NH:
                    act.wait_ge(na["biased"], n + 1)
                    for r in range(2):
                        e = nc.scalar.activation(at["s"][:, n % 3, r, :], at["s"][:, n % 3, r, :], ACT.Exp,
                                                 bias=at["mx"][:, n % 3, r:r + 1],
                                                 accum_out=at["sm"][:, n % 3, r:r + 1])
                    e.then_inc(na["exp"], 1)

        def hyena():
            def magnitudes_of(n):
                act.wait_ge(hs["ab"], n + 1)
                for part in range(2):
                    ab = nc.scalar.activation(hy["H"][:, n % 2, 2 * part:2 * part + 2, :], filter_parts(n)[part],
                                              ACT.Abs)
                ab.then_inc(hs["abs"], 1)

            def filter_spectra(n, rows):
                act.wait_ge(hs["am"], n + 1)
                for i in rows:
                    act.wait_ge(hs["Hps"], 5 * n + i + 1)
                    nc.scalar.copy(hy["H"][:, n % 2, i, :], spectrum_bank(n, i)[:]).then_inc(hs["H"], 1)

            tap = first_taps(PH["in2"], 0, 16)
            for j in range(4):
                tap(4, j, K8)
                if j == 1:
                    magnitudes_of(0)
            for j, rows in enumerate(((), (0, 1, 2), (3, 4), ())):
                tap(5, j, K8)
                if rows:
                    filter_spectra(0, rows)
            for n in range(4):
                act.wait_ge(hs["turned"], n + 1)
                nc.scalar.copy(hy["ut"][:, 0, :], bank[0][:])
                nc.scalar.copy(hy["ut"][:, 1, :], bank[3][:]).then_inc(hs["ut"], 1)
                if n < 3:
                    magnitudes_of(n + 1)
                    filter_spectra(n + 1, range(5))

        def decay(h):
            back = rt["tab"][:, RTAB["back"]:RTAB["back"] + 3 * L]
            ahead = rt["tab"][:, RTAB["ahead"]:RTAB["ahead"] + 3 * L]
            if h >= 2:
                act.wait_ge(re["sd"], h - 1)
            nc.scalar.activation(rt["e1"][:, h % 2].rearrange("p a b -> p (a b)"), back, ACT.Exp,
                                 scale=rt["lg"][:, 0, h:h + 1])
            if h:
                act.wait_ge(re["d"], h)
            nc.scalar.activation(rt["e2"][:].rearrange("p a b -> p (a b)"), ahead, ACT.Exp,
                                 scale=rt["lg"][:, 1, h:h + 1]).then_inc(re["e"], 1)

        def first_decays():
            act.wait_ge(re["loaded"], 32)
            nc.scalar.activation(rt["lg"][:], rt["dec"][:], ACT.Exp).then_inc(re["lg"], 1)
            act.wait_ge(re["lg"], 2)
            decay(0)
            decay(1)

        def retention():
            act.wait_ge(bank_free, tiles_out(PH["in_ret"]))
            act.wait_ge(re["loaded"], 32)
            for m in range(8):
                nc.scalar.activation(rt["t"][:, 16 + m, :], rt["t"][:, 16 + m, :], ACT.Silu).then_inc(re["silu"], 1)
            for i in range(8):
                act.wait_ge(re["vps"], i + 1)
                nc.scalar.copy(rt["vt"][:, 0:2, i * P:(i + 1) * P],
                               bank[6 + i % 2][:, 0:2 * P].rearrange("p (a b) -> p a b", a=2))
                nc.scalar.copy(rt["vt"][0:JT[2][1], 2, i * P:(i + 1) * P],
                               bank[6 + i % 2][0:JT[2][1], 2 * P:3 * P]).then_inc(re["vt"], 1)

            def variance(h):
                act.wait_ge(re["vps2"], h + 1)
                nc.scalar.activation(rt["var"][:, h, :], bank[6 + h % 2][:, B], ACT.Identity, bias=eps[:, 1:2],
                                     scale=1.0 / RDV).then_inc(re["var"], 1)

            def inverse_deviation(half):
                act.wait_ge(re["var"], RH // 2 * (half + 1))
                var = rt["var"][:, RH // 2 * half:RH // 2 * (half + 1), :]
                link(nc.scalar.activation(var, var, ACT.Ln))
                nc.scalar.activation(var, var, ACT.Exp, scale=-0.5).then_inc(re["rr"], 1)

            for t in range(RH + 6):
                h = t - 2
                if 0 <= h < RH:
                    act.wait_ge(re["yps"], h + 1)
                    if h >= 2:
                        act.wait_ge(re["centred"], h - 1)
                    nc.scalar.copy(silu[:, h % 2, :], bank[3 + h % 2][:, B]).then_inc(re["y"], 1)
                h = t - 4
                if 0 <= h < RH:
                    act.wait_ge(re["centred"], h + 1)
                    nc.scalar.copy(rt["yc"][:, h, :], bank[5][:, B]).then_inc(re["yc"], 1)
                    act.wait_ge(re["yc"], h + 1)
                    if h >= 2:
                        act.wait_ge(re["vps2"], h - 1)
                    nc.scalar.activation(gate[:, h % 2, :], rt["yc"][:, h, :], ACT.Square).then_inc(re["squared"], 1)
                h = t - 6
                if 0 <= h < RH:
                    variance(h)
                if t + 2 < RH:
                    decay(t + 2)
                if t == RH + 3:
                    inverse_deviation(0)
            ph = PH["in_mla"]
            split_hi(ph, 0, 0, 0, K8)
            inverse_deviation(1)
            for j in range(1, 6):
                split_hi(ph, 0, j // 4, j % 4, K8)

        def latent():
            ph = PH["in_gate"]
            for j in range(4):
                split_hi(ph, 0, 0, j, K8)
            act.wait_ge(bank_free, tiles_out(PH["in_mla"]))
            act.wait_ge(y_lo, YBASE["ret"] + RH)
            groups = ((0, QR // P), (QR // P, KR // P))
            for g, (c0, cn) in enumerate(groups):
                if g:
                    split_hi(ph, 0, 1, 0, K8)
                    act.wait_ge(ms["sums"], 1)
                nc.scalar.activation(ml["sq"][:, 0:cn, :], ml["c"][:, c0:c0 + cn, :],
                                     ACT.Square).then_inc(ms["squared"], 1)
            split_hi(ph, 0, 1, 1, K8)
            for g, (c0, cn) in enumerate(groups):
                act.wait_ge(ms["sums"], g + 1)
                link(nc.scalar.activation(ml["rr"][:, g, :], bank[4 + g][:, B], ACT.Ln, bias=eps[:, 0:1],
                                          scale=1.0 / (cn * P)))
            for g in range(2):
                nc.scalar.activation(ml["rr"][:, g, :], ml["rr"][:, g, :], ACT.Exp, scale=-0.5).then_inc(ms["rr"], 1)
            for j in range(2, 4):
                split_hi(ph, 0, 1, j, K8)
            only_split(ph, 8, 8)
            for r, (t0, tn) in enumerate(JT):
                act.wait_ge(ms["vps"], r + 1)
                nc.scalar.copy(ml["vt"][0:tn, r, :], bank[4 + r][0:tn, :]).then_inc(ms["vt"], 1)

            def turned(h, r):
                tn = JT[r][1]
                act.wait_ge(ms["turned"], 3 * h + r + 1)
                nc.scalar.copy(ml["pt"][0:tn, h % 2, r, :],
                               bank[6 + r % 2][0:tn, B]).then_inc(ms[("pt0", "pt1", "pt")[r]], 1)

            for t in range(MH + 3):
                h = t
                if h < MH:
                    act.wait_ge(ms["qps"], h + 1)
                    if h:
                        act.wait_ge(ms["q"], h)
                    nc.scalar.copy(ml["qraw"][0:MQK, :], bank[0][0:MQK, B]).then_inc(ms["qraw"], 1)
                    act.wait_ge(ms["kps"], h + 1)
                    if h >= 2:
                        act.wait_ge(ms["scores"], h - 1)
                    nc.scalar.copy(ml["k"][NOPE:MQK, h % 2, :], ml["kr"][NOPE:MQK, :])
                    nc.scalar.copy(ml["k"][0:NOPE, h % 2, :], bank[0][0:NOPE, B]).then_inc(ms["k"], 1)
                h = t - 3
                if 0 <= h < MH:
                    if h >= 2:
                        act.wait_ge(ms["out"], h - 1)
                    turned(h, 0)
                    turned(h, 1)
                h = t - 1
                if 0 <= h < MH:
                    act.wait_ge(ms["max"], h + 1)
                    if h >= 3:
                        act.wait_ge(ms["turned"], 3 * (h - 2))
                    for r, (t0, tn) in enumerate(JT):
                        e = nc.scalar.activation(ml["s"][0:tn, h % 3, r, :], bank[3 + r][0:tn, B], ACT.Exp,
                                                 bias=ml["mx"][0:tn, h % 3, r:r + 1], scale=MQK ** -0.5,
                                                 accum_out=ml["sm"][0:tn, h % 3, r:r + 1])
                    e.then_inc(ms["exp"], 1)
                h = t - 3
                if 0 <= h < MH:
                    turned(h, 2)
            act.wait_ge(bank_free, tiles_out(ph))
            for half in range(2):
                g = ml["g"][:, 8 * half:8 * half + 8, :]
                nc.scalar.activation(g, g, ACT.Sigmoid).then_inc(gate_on, 1)

        act.wait_ge(eps_set, 1)
        act.wait_ge(start_loaded, 64)
        nc.scalar.activation(cm["cv"][:], x[:, :, A], ACT.Square).then_inc(first_squares, 1)

        def filter_sine(layer):
            act.wait_ge(filt_arg, layer + 1)
            nc.scalar.activation(filt_hid[:], filt_x[:], ACT.Sin).then_inc(filt_sin, 1)

        for p in range(RING):
            act.wait_ge(loaded[p], 16)
            nc.scalar.copy(whi[:, p, 0:K8 * P], raw[:, p, 0:K8 * P]).then_inc(panel_hi, 1)
        norm = 0
        for layer, kind in enumerate(KINDS):
            ph = PH[f"in{layer}"]
            norm_root(norm, A)
            norm += 1
            if kind == "conv":
                only_split(ph, 0, 8)
                if layer == 0:
                    filter_sine(0)
                first_taps(ph, 8, 8)
                y_high(ph, 16, 8, cm["yh"], A, YR[f"in{layer}"])
                if layer == 0:
                    filter_sine(1)
            elif kind == "attention":
                attention()
            else:
                hyena()
            only_split(PH[f"out{layer}"])
            norm_root(norm, A)
            norm += 1
            gates(PH[f"up{layer}"], layer, A)
            only_split(PH[f"down{layer}"])
        norm_root(norm, B)
        norm += 1
        only_split(PH["in_ret"], 0, 16)
        first_decays()
        only_split(PH["in_ret"], 16, 8)
        retention()
        latent()

        only_split(PH["ret_out"])

        ph_mo = PH["mla_out"]
        for j in range(4):
            for u in range(2):
                m = 2 * j + u
                act.wait_ge(y_ready, YR["mrg"] + m + 1)
                nc.scalar.copy(mg["yh2"][:, m, :], hid[:, u, :]).then_inc(y_hi, 1)
            split_hi(ph_mo, 0, 0, j, K8)
        only_split(PH["w_o"])
        norm_root(norm, B)
        norm += 1
        gates(PH["up4"], DEPTH, B)
        only_split(PH["down4"])
        norm_root(norm, B)

    @block.gpsimd
    def _(pool):
        link = Chain(pool, pool_chain)
        pool.wait_ge(start_loaded, 64)

        def decay_products():
            for h in range(RH):
                pool.wait_ge(re["e"], h + 1)
                e1 = rt["e1"][:, h % 2].rearrange("p a b -> p (a b)")
                nc.gpsimd.tensor_tensor(e1, e1, rt["e2"][:].rearrange("p a b -> p (a b)"),
                                        ALU.mult).then_inc(re["d"], 1)

        def mask_bias():
            pool.wait_ge(bias_loaded, 16)
            bias = at["bias"][:].rearrange("p h j k -> p (h j) k")
            mask = k_("colmask", GW).unsqueeze(1).broadcast_to([P, NH * 6, GW])
            nc.gpsimd.tensor_tensor(bias, bias, mask, ALU.add).then_inc(bias_masked, 1)

        def newton_products():
            for g in range(4):
                pool.wait_ge(na["rr2"], g + 1)
                nw = an["nw"][:, g % 2]
                nc.gpsimd.tensor_tensor(nw, nw, an["ms"][:, 4 * g:4 * g + 4, :], ALU.mult).then_inc(na["near_one"], 1)

        for norm in range(1, NORMS):
            cols = A if norm < 2 * DEPTH else B
            if norm == 3:
                mask_bias()
                newton_products()
            if norm == 2 * DEPTH + 1:
                decay_products()
            if norm == NORMS - 1:
                s, base = bank_free, PH["down4"].t0 + 4
            else:
                s, base = x_hi, C * norm
            pool.wait_ge(s, base + 1)
            link(nc.gpsimd.tensor_tensor(sumsq[:, cols], x[:, 0, cols], x[:, 0, cols], ALU.mult))
            start = link.n
            with pool.Fori(1, C) as m:
                link.n = start + 2 * (m - 1)
                pool.wait_ge(s, base + 1 + m)
                link(nc.gpsimd.tensor_tensor(square[:, cols], x[:, m, cols], x[:, m, cols], ALU.mult))
                link(nc.gpsimd.tensor_tensor(sumsq[:, cols], sumsq[:, cols], square[:, cols], ALU.add))
            link.n = start + 2 * (C - 1)
            nc.gpsimd.memset(square[:, 0:2], 0.0).then_inc(sumsq_done, 1)

    def dve_steps(*args):
        steps(nc.vector, *args, ahead=3)

    @block.vector
    def _(dve):
        link = Chain(dve, dve_chain)
        V = nc.vector

        def split_lo(ph, first, i, j, k):
            if k is None:
                return
            p = ph.p0 + first + j + 3
            dve.wait_ge(panel_hi, p + 1 + 4 * i)
            V.tensor_tensor(wlo[:, p % RING, 0:k * P], raw[:, p % RING, 0:k * P],
                            whi[:, p % RING, 0:k * P].bitcast(F32), ALU.subtract).then_inc(panel_lo, 1)

        def norm_inv(norm, cols):
            dve.wait_ge(root_ready, norm + 1)
            V.tensor_scalar(mean_sq[:, cols], bank[7][:, cols], 1.0 / D, EPS, ALU.mult, ALU.add)
            link(V.reciprocal(rinv[:, cols], root[:, cols]))
            link(V.tensor_tensor(newton[:, cols], rinv[:, cols], rinv[:, cols], ALU.mult))
            link(V.tensor_tensor(newton[:, cols], newton[:, cols], mean_sq[:, cols], ALU.mult))
            link(V.tensor_scalar(newton[:, cols], newton[:, cols], -0.5, 1.5, ALU.mult, ALU.add))
            V.tensor_tensor(rinv[:, cols], rinv[:, cols], newton[:, cols], ALU.mult).then_inc(rinv_ready, 1)
            dve.wait_ge(rinv_ready, norm + 1)

        def x_parts(m, gain, cols, norm):
            V.tensor_scalar(xh[:, m, cols], x[:, m, cols], gain, None, ALU.mult).then_inc(x_hi, 1)
            dve.wait_ge(x_hi, C * norm + m + 1)
            V.scalar_tensor_tensor(out=xl[:, m, cols], in0=x[:, m, cols], scalar=gain,
                                   in1=xh[:, m, cols].bitcast(F32), op0=ALU.mult,
                                   op1=ALU.subtract).then_inc(x_lo, 1)

        def residual(ph, gain, cols, norm, next_cols):
            w = slice(0, cols.stop - cols.start)

            def step(i, j, k):
                half = ph.k == K11
                m = j // 2 + 2 * i if half else j + 4 * i
                tile = (ph.t0 + (j // 2 if half else j)) - ph.t0
                if not half or j % 2:
                    dve.wait_ge(panel_used, ph.p0 + j + 1 + 4 * i)
                    V.tensor_tensor(x[:, m, cols], x[:, m, cols], bank[(ph.b0 + tile) % 4][:, w],
                                    ALU.add).then_inc(bank_free, 1)
                    if norm < NORMS - 1:
                        dve.wait_ge(bank_free, ph.t0 + m + 5)
                        x_parts(m, v(gain[0], gain[1] + m), next_cols, norm)
                split_lo(ph, 0, i, j, k)
            dve_steps(ph, 0, ph.n, step)

        def scaled(ph, first, n, dst, keep=None):
            def step(i, j, k):
                m = j + 4 * i
                t = ph.t0 + first + j
                dve.wait_ge(panel_used, ph.p0 + first + j + 1 + 4 * i)
                d = dst(j, m)
                cols = A if d.shape[-1] == SEQ else B
                V.tensor_tensor(d, bank[(ph.b0 + first + j) % 4][:, 0:d.shape[-1]], rinv[:, cols],
                                ALU.mult).then_inc(bank_free, 1)
                if keep is not None:
                    dve.wait_ge(bank_free, t + 5 + 4 * i)
                    keep(j, m)
                split_lo(ph, first, i, j, k)
            return step

        def feed_forward(ph, index, cols):
            w = slice(0, cols.stop - cols.start)
            g0 = index * FC

            def low(i, s):
                dve.wait_ge(hid_hi, g0 + s + 1 + 2 * i)
                V.tensor_tensor(ffn["hl"][:, s + 2 * i, cols], hid[:, s, w],
                                ffn["hh"][:, s + 2 * i, cols].bitcast(F32), ALU.subtract).then_inc(hid_lo, 1)

            def step(i, j, k):
                s = j // 2
                dve.wait_ge(panel_used, ph.p0 + j + 1 + 4 * i)
                ps = bank[(ph.b0 + j) % 4][:, w]
                if j % 2 == 0:
                    V.tensor_tensor(gate[:, s, w], ps, rinv[:, cols], ALU.mult).then_inc(bank_free, 1)
                    split_lo(ph, 0, i, j, k)
                    if j == 2:
                        low(i, 0)
                    return
                V.tensor_tensor(up[:, s, w], ps, rinv[:, cols], ALU.mult).then_inc(bank_free, 1)
                dve.wait_ge(bank_free, ph.t0 + j + 5 + 4 * i)
                dve.wait_ge(gate_silu, g0 + s + 1 + 2 * i)
                V.tensor_tensor(hid[:, s, w], silu[:, s, w], up[:, s, w], ALU.mult).then_inc(hid_ready, 1)
                split_lo(ph, 0, i, j, k)
                if j == 3:
                    low(i, 1)
            dve_steps(ph, 0, ph.n, step)

        def short_conv(layer):
            ph, ai = PH[f"in{layer}"], layer // 3
            link(V.memset(cm["cu"][:], 0.0))
            dve_steps(ph, 0, 8, scaled(ph, 0, 8, lambda j, m: cm["c"][:, m, :]))
            if layer == 0:
                filter_argument(0)

            def conv_step(i, j, k):
                m = j + 4 * i
                cu, cv = cm["cu"][:, j % 2], cm["cv"][:, m, :]
                w = VEC["a_conv"] + ai * 3 * C
                dve.wait_ge(panel_used, ph.p0 + 8 + j + 1 + 4 * i)
                V.tensor_tensor(up[:, j % 2, 0:SEQ], bank[(ph.b0 + j) % 4][:, 0:SEQ], rinv[:, A],
                                ALU.mult).then_inc(bank_free, 1)
                dve.wait_ge(bank_free, ph.t0 + 8 + j + 5 + 4 * i)
                V.tensor_tensor(cu[:, 1:SEQ + 1], up[:, j % 2, 0:SEQ], cm["c"][:, m, :], ALU.mult).then_inc(conv_in, 1)
                split_lo(ph, 8, i, j, k)
                dve.wait_ge(first_tap, TAPS[ph.name] + j + 1 + 4 * i)
                for t in (1, 2):
                    link(V.scalar_tensor_tensor(out=cv, in0=cu[:, t:t + SEQ], scalar=vec[:, bass.ds(w + t * C + m, 1)],
                                                in1=cv, op0=ALU.mult, op1=ALU.add))
            dve_steps(ph, 8, 8, conv_step, link, 8)

            ready0, y0 = YR[f"in{layer}"], YBASE[f"in{layer}"]

            def step(i, j, k):
                m = j + 4 * i
                dve.wait_ge(panel_used, ph.p0 + 16 + j + 1 + 4 * i)
                V.tensor_tensor(up[:, j % 2, 0:SEQ], bank[(ph.b0 + j) % 4][:, 0:SEQ], rinv[:, A],
                                ALU.mult).then_inc(bank_free, 1)
                dve.wait_ge(bank_free, ph.t0 + 16 + j + 5 + 4 * i)
                V.tensor_tensor(hid[:, j % 2, 0:SEQ], up[:, j % 2, 0:SEQ], cm["cv"][:, m, :],
                                ALU.mult).then_inc(y_ready, 1)
                split_lo(ph, 16, i, j, k)
                dve.wait_ge(y_hi, y0 + m + 1)
                V.tensor_tensor(cm["yl"][:, m, A], hid[:, j % 2, 0:SEQ], cm["yh"][:, m, A].bitcast(F32),
                                ALU.subtract).then_inc(y_lo, 1)
            dve_steps(ph, 16, 8, step)

        def y_from_bank(bufs, c, ps, cols, y0):
            V.tensor_copy(bufs["yh"][:, c, cols], ps).then_inc(y_hi, 1)
            dve.wait_ge(y_hi, y0 + c + 1)
            V.tensor_tensor(bufs["yl"][:, c, cols], ps, bufs["yh"][:, c, cols].bitcast(F32),
                            ALU.subtract).then_inc(y_lo, 1)

        def attention():
            ph = PH["in1"]
            dve_steps(ph, 0, 16, scaled(ph, 0, 16, lambda j, m: at["qkv"][:, m, :]))
            value = scaled(ph, 16, 8, lambda j, m: at["qkv"][:, 16 + m, :])
            value(0, 0, K8)
            value(0, 1, K8)
            value(0, 2, K8)
            for g in range(4):
                value(0 if g == 0 else 1, (3 + g) % 4, K8)
                dve.wait_ge(na["near_one"], g + 1)
                rr = an["rr"][:, 4 * g:4 * g + 4, :]
                nw = an["nw"][:, g % 2]
                V.scalar_tensor_tensor(out=rr, in0=nw, scalar=-3.0, in1=rr, op0=ALU.add,
                                       op1=ALU.mult).then_inc(na["newton"], 1)
                dve.wait_ge(na["newton"], g + 1)
                w = slice(4 * g, 4 * g + 4)
                V.scalar_tensor_tensor(out=at["qkv"][:, w, :], in0=at["qkv"][:, w, :], scalar=v(("q_g", "k_g")[g // 2]),
                                       in1=rr, op0=ALU.mult, op1=ALU.mult).then_inc(na["qk"], 1)
            value(1, 3, K8)
            dve.wait_ge(bias_masked, 1)
            dve.wait_ge(na["qk"], 4)
            for t in range(NH + 6):
                n = t
                if 0 <= n < NH:
                    dve.wait_ge(na["scores"], n + 1)
                    if n >= 3:
                        dve.wait_ge(na["turned"], n - 2)
                    for r in range(2):
                        b = at["bias"][:, n, 2 - 2 * r:6 - 2 * r, :].rearrange("p j k -> p (j k)")
                        e = V.scalar_tensor_tensor(out=at["s"][:, n % 3, r, :],
                                                   in0=bank[4 + n % 2][:, r * SEQ:(r + 1) * SEQ],
                                                   scalar=0.25 * HD ** -0.5, in1=b, op0=ALU.mult, op1=ALU.add)
                    link(e)
                    link(V.tensor_reduce(at["mx"][:, n % 3, :], at["s"][:, n % 3], AXX, ALU.max))
                    V.tensor_scalar(at["mx"][:, n % 3, :], at["mx"][:, n % 3, :], -1.0, None,
                                    ALU.mult).then_inc(na["biased"], 1)
                n = t - 1
                if 0 <= n < NH:
                    dve.wait_ge(na["exp"], n + 1)
                    link(V.reciprocal(at["rs"][:, n % 3, :], at["sm"][:, n % 3, :]))
                    for r in range(2):
                        e = V.tensor_scalar(at["s"][:, n % 3, r, :], at["s"][:, n % 3, r, :],
                                            at["rs"][:, n % 3, r:r + 1], None, ALU.mult)
                    e.then_inc(na["p"], 1)
                n = t - 5
                if 0 <= n < NH and n % 2:
                    dve.wait_ge(na["out"], n + 1)
                    y_from_bank(at, n // 2, bank[2 + n // 2 % 2][:, 0:SEQ], A, YBASE["in1"])

        def hyena():
            ph = PH["in2"]
            link(V.memset(hy["rawz"][:], 0.0))

            def conv_step(i, j, k):
                m = j + 4 * i
                rz, z = hy["rawz"][:, j % 2], hy["z"][:, m, :]
                dve.wait_ge(panel_used, ph.p0 + j + 1 + 4 * i)
                V.tensor_tensor(rz[:, 1:SEQ + 1], bank[(ph.b0 + j) % 4][:, 0:SEQ], rinv[:, A],
                                ALU.mult).then_inc(bank_free, 1)
                split_lo(ph, 0, i, j, k)
                dve.wait_ge(first_tap, TAPS["in2"] + j + 1 + 4 * i)
                for t in (1, 2):
                    link(V.scalar_tensor_tensor(out=z, in0=rz[:, t:t + SEQ],
                                                scalar=vec[:, bass.ds(VEC["c_conv"] + t * 24 + m, 1)], in1=z,
                                                op0=ALU.mult, op1=ALU.add))
            dve_steps(ph, 0, 16, conv_step, link, 8)

            def decayed(n):
                dve.wait_ge(hs["F"], n + 1)
                for d in range(2):
                    for r in range(2):
                        e = V.tensor_tensor(hy["frY"][:, 2 * d + r, :], bank[4 + 2 * d + r][:], hy["decay"][:, r, :],
                                            ALU.mult)
                e.then_inc(hs["fr"], 1)

            def filters(n):
                fr = hy["frY"]
                dve.wait_ge(hs["fr"], n + 1)
                if n:
                    dve.wait_ge(hs["Hps"], 5 * n)
                for part, op in enumerate((ALU.add, ALU.subtract)):
                    e = V.tensor_tensor(filter_parts(n)[part], fr[:, 0:2, :], fr[:, 2:4, :], op)
                e.then_inc(hs["ab"], 1)

            def filter_magnitudes(n):
                dve.wait_ge(hs["abs"], n + 1)
                H = hy["H"][:, n % 2]
                link(V.tensor_tensor(magnitudes(n), H[:, 0:2, :], H[:, 2:4, :], ALU.max))
                V.tensor_copy(magnitudes(n)[0:1, 0, :], H[0:1, 0, :]).then_inc(hs["am"], 1)

            def inverse_sum(n):
                dve.wait_ge(hs["norm"], n + 1)
                V.reciprocal(hy["inv"][:, n % 2, :], sum_bank(n)[:, 0:HJ]).then_inc(hs["inv"], 1)

            decayed(0)
            for j in range(8):
                conv_step(4 + j // 4, j % 4, K8)
                if j == 0:
                    filters(0)
                elif j == 3:
                    filter_magnitudes(0)
                elif j == 6:
                    inverse_sum(0)
            for n in range(4):
                half, order = n // 2, n % 2
                if n < 3:
                    decayed(n + 1)
                    filters(n + 1)
                    filter_magnitudes(n + 1)
                H, Yv = hy["H"][:, n % 2], hy["frY"]
                dve.wait_ge(hs["H"], 5 * n + 5)
                link(V.memset(H[0:1, 2, :], 0.0))
                for f in range(2):
                    if f and n < 3:
                        inverse_sum(n + 1)
                    dve.wait_ge(hs["U"], 2 * n + f + 1)
                    ur, us = bank[4 + f][:], bank[6 + f][:]
                    hc, hsn, hx = H[:, f, :], H[:, 2 + f, :], H[:, 4 if f == 0 else 1, :]
                    V.tensor_tensor(Yv[:, f, :], ur, hc, ALU.mult)
                    link(V.tensor_tensor(hy["t1"][:], us, hsn, ALU.mult))
                    link(V.tensor_tensor(Yv[:, f, :], Yv[:, f, :], hy["t1"][:], ALU.subtract))
                    V.tensor_tensor(Yv[:, 2 + f, :], us, hx, ALU.mult)
                    link(V.tensor_tensor(hy["t1"][:], ur, hsn, ALU.mult))
                    e = V.tensor_tensor(Yv[:, 2 + f, :], Yv[:, 2 + f, :], hy["t1"][:], ALU.add)
                    if f == 0:
                        link(e)
                e.then_inc(hs["Y"], 1)
                for j in range(HJ):
                    cc = half * HJ + j
                    t = up[:, j % 2, 0:SEQ]
                    z = hy["z"]
                    link(V.tensor_scalar(t, z[:, cc, :], v("c_skip", order * C + cc), None, ALU.mult))
                    dve.wait_ge(hs["inv"], n + 1)
                    dve.wait_ge(hs["back"], 4 * n + j + 1)
                    link(V.scalar_tensor_tensor(out=t, in0=bank[j][:, 0:SEQ], scalar=hy["inv"][:, n % 2, j:j + 1],
                                                in1=t, op0=ALU.mult, op1=ALU.add))
                    dst = z[:, cc, :] if order == 0 else hid[:, j % 2, 0:SEQ]
                    V.tensor_tensor(dst, z[:, 8 * (order + 1) + cc, :], t, ALU.mult).then_inc(hs["z"], 1)
                    dve.wait_ge(hs["z"], 4 * n + j + 1)
                    if order:
                        y_from_bank(hy, cc, dst, A, YBASE["in2"])

        def retention():
            ph = PH["in_ret"]
            dve_steps(ph, 0, 16, scaled(ph, 0, 16, lambda j, m: rt["t"][:, m, :]))
            dve.wait_ge(re["lg"], 1)
            V.tensor_scalar(rt["lg"][:], rt["lg"][:], -1.0, None, ALU.mult).then_inc(re["lg"], 1)
            dve_steps(ph, 16, 8, scaled(ph, 16, 8, lambda j, m: rt["t"][:, 16 + m, :]))
            dve.wait_ge(re["loaded"], 32)
            cos, sin = (rt["tab"][:, RTAB[s]:RTAB[s] + L] for s in ("cos", "sin"))
            for i in range(8):
                dve.wait_ge(re["rot"], i + 1)
                t = rt["t"][:, i, :]
                V.tensor_tensor(t, t, cos, ALU.mult)
                link(V.tensor_tensor(up[:, 0, :], bank[4 + i % 2][:, B], sin, ALU.mult))
                V.tensor_tensor(t, t, up[:, 0, :], ALU.add).then_inc(re["roped"], 1)
                dve.wait_ge(re["roped"], i + 1)
            for h in range(RH):
                dve.wait_ge(re["scores"], h + 1)
                dve.wait_ge(re["d"], h + 1)
                if h >= 2:
                    dve.wait_ge(re["yps"], h - 1)
                for r, (t0, tn) in enumerate(JT):
                    e = V.scalar_tensor_tensor(out=rt["sd"][0:tn, h % 2, r, :], in0=bank[r][0:tn, B],
                                               scalar=RDK ** -0.5, in1=rt["e1"][0:tn, h % 2, r, :],
                                               op0=ALU.mult, op1=ALU.mult)
                e.then_inc(re["sd"], 1)

        def retention_out():
            ph = PH["in_mla"]
            step = scaled(ph, 0, 6, lambda j, m: ml["c"][:, m, :])
            ph_gate = PH["in_gate"]
            gate_step = scaled(ph_gate, 0, 8, lambda j, m: ml["g"][:, m, :])
            dve.wait_ge(re["silu"], 8)
            for h in range(RH):
                if h < 6:
                    step(h // 4, h % 4, K8)
                else:
                    gate_step(0, h - 6, K8)
                if h % (RH // 2) == 0:
                    dve.wait_ge(re["rr"], h // (RH // 2) + 1)
                link(V.tensor_tensor(up[:, 1, :], rt["yc"][:, h, :], rt["var"][:, h, :], ALU.mult))
                link(V.scalar_tensor_tensor(out=hid[:, h % 2, :], in0=up[:, 1, :], scalar=v("gn_w", h),
                                            in1=rt["t"][:, 16 + h, :], op0=ALU.mult, op1=ALU.mult))
                y_from_bank(rt, h, hid[:, h % 2, :], B, YBASE["ret"])
            gate_step(0, 2, K8)
            gate_step(0, 3, K8)

        def latent():
            dve.wait_ge(ms["loaded"], 64)
            gate_step = scaled(PH["in_gate"], 0, 8, lambda j, m: ml["g"][:, m, :])
            gate_step(1, 0, K8)
            gate_step(1, 1, K8)
            for g, (c0, cn, gain) in enumerate(((0, QR // P, "q_norm"), (QR // P, KR // P, "kv_norm"))):
                dve.wait_ge(ms["rr"], g + 1)
                rr = ml["rr"][:, g, :]
                link(V.tensor_scalar(ml["ms"][:], bank[4 + g][:, B], 1.0 / (cn * P), EPS, ALU.mult, ALU.add))
                link(V.tensor_tensor(ml["nw"][:], rr, rr, ALU.mult))
                link(V.tensor_tensor(ml["nw"][:], ml["nw"][:], ml["ms"][:], ALU.mult))
                link(V.tensor_scalar(ml["nw"][:], ml["nw"][:], -0.5, 1.5, ALU.mult, ALU.add))
                link(V.tensor_tensor(rr, rr, ml["nw"][:], ALU.mult))
                for i in range(cn):
                    c = ml["c"][:, c0 + i, :]
                    e = V.scalar_tensor_tensor(out=c, in0=c, scalar=v(gain, i), in1=ml["rr"][:, g, :], op0=ALU.mult,
                                               op1=ALU.mult)
                e.then_inc(ms["normed"], 1)
                gate_step(1, g + 2, K8)
            cos, sin = (ml["tab"][0:MQK, MTAB[s]:MTAB[s] + L] for s in ("cos", "sin"))
            rope = slice(NOPE, MQK)
            dve.wait_ge(ms["krot"], 1)
            V.tensor_tensor(ml["kr"][rope, :], ml["c"][rope, 5, :], cos[rope, :], ALU.mult)
            link(V.tensor_tensor(up[rope, 0, :], bank[6][rope, B], sin[rope, :], ALU.mult))
            V.tensor_tensor(ml["kr"][rope, :], ml["kr"][rope, :], up[rope, 0, :], ALU.add).then_inc(ms["kr"], 1)
            dve_steps(PH["in_gate"], 8, 8, scaled(PH["in_gate"], 8, 8, lambda j, m: ml["g"][:, 8 + m, :]))
            for t in range(MH + 5):
                h = t - 5
                if 0 <= h < MH and h % 2:
                    dve.wait_ge(ms["out"], h + 1)
                    y_from_bank(ml, h // 2, bank[2][:, B], B, YBASE["mla"])
                h = t - 2
                if 0 <= h < MH:
                    dve.wait_ge(ms["exp"], h + 1)
                    for r, tn in ((0, P), (2, JT[2][1])):
                        s = slice(0, 2) if r == 0 else slice(2, 3)
                        link(V.reciprocal(ml["rs"][0:tn, h % 3, s], ml["sm"][0:tn, h % 3, s]))
                    for r, (t0, tn) in enumerate(JT):
                        s = ml["s"][0:tn, h % 3, r, :]
                        e = V.tensor_scalar(s, s, ml["rs"][0:tn, h % 3, r:r + 1], None, ALU.mult)
                    e.then_inc(ms["p"], 1)
                h = t
                if h < MH:
                    q = ml["q"][0:MQK, h % 2, :]
                    dve.wait_ge(ms["qraw"], h + 1)
                    if h >= 2:
                        dve.wait_ge(ms["scores"], h - 1)
                    V.tensor_tensor(q, ml["qraw"][0:MQK, :], cos, ALU.mult)
                    dve.wait_ge(ms["rot"], h + 1)
                    link(V.tensor_tensor(up[0:MQK, 0, :], bank[1][0:MQK, B], sin, ALU.mult))
                    V.tensor_tensor(q, q, up[0:MQK, 0, :], ALU.add).then_inc(ms["q"], 1)
                h = t - 1
                if 0 <= h < MH:
                    dve.wait_ge(ms["scores"], h + 1)
                    for r, (t0, tn) in enumerate(JT):
                        e = V.tensor_reduce(ml["mx"][0:tn, h % 3, r:r + 1], bank[3 + r][0:tn, B], AXX, ALU.max)
                    link(e)
                    V.tensor_scalar(ml["mx"][:, h % 3, 0:2], ml["mx"][:, h % 3, 0:2], -MQK ** -0.5, None, ALU.mult)
                    V.tensor_scalar(ml["mx"][0:JT[2][1], h % 3, 2:3], ml["mx"][0:JT[2][1], h % 3, 2:3], -MQK ** -0.5,
                                    None, ALU.mult).then_inc(ms["max"], 1)

        V.memset(eps[:, 0:1], EPS)
        V.memset(eps[:, 1:2], GN_EPS).then_inc(eps_set, 1)
        V.memset(gate[:, 0, 0:2], 0.0).then_inc(bank_free, 4)
        dve.wait_ge(start_loaded, 64)
        for m in range(C):
            x_parts(m, v("mix_g", m), A, 0)
            if m in (3, 5, 7):
                p = m // 2 - 1
                dve.wait_ge(panel_hi, p + 1)
                V.tensor_tensor(wlo[:, p, 0:K8 * P], raw[:, p, 0:K8 * P], whi[:, p, 0:K8 * P].bitcast(F32),
                                ALU.subtract).then_inc(panel_lo, 1)

        def filter_argument(layer):
            dve.wait_ge(filt_ps, layer + 1)
            F_, S_ = slice(0, FHID), slice(0, SEQ)
            arg, turns, r = up[F_, 0, S_], up[F_, 1, S_], filt_x[:]
            bias = v(("f_b1", "f_b2")[layer])[F_, :]
            link(V.tensor_scalar(arg, bank[6][F_, S_], bias, v("f_freq")[F_, :], ALU.add, ALU.mult))
            link(V.tensor_scalar(turns, arg, 1 / (2 * math.pi), ROUND, ALU.mult, ALU.add))
            link(V.tensor_scalar(turns, turns, -ROUND, None, ALU.add))
            link(V.scalar_tensor_tensor(out=arg, in0=turns, scalar=-TWO_PI_HI, in1=arg, op0=ALU.mult, op1=ALU.add))
            link(V.scalar_tensor_tensor(out=arg, in0=turns, scalar=-TWO_PI_LO, in1=arg, op0=ALU.mult, op1=ALU.add))
            V.tensor_scalar(r, arg, PI_IN, -PI_IN, ALU.min, ALU.max).then_inc(filt_arg, 1)
            dve.wait_ge(filt_arg, layer + 1)

        norm = 0
        for layer, kind in enumerate(KINDS):
            norm_inv(norm, A)
            norm += 1
            if kind == "conv":
                short_conv(layer)
                if layer == 0:
                    filter_argument(1)
            elif kind == "attention":
                attention()
            else:
                hyena()
            residual(PH[f"out{layer}"], ("ffn_g", layer * C), A, norm, A)
            norm_inv(norm, A)
            norm += 1
            feed_forward(PH[f"up{layer}"], layer, A)
            last = layer == DEPTH - 1
            residual(PH[f"down{layer}"], ("mix_w2", 0) if last else ("mix_g", (layer + 1) * C), A, norm,
                     B if last else A)
        norm_inv(norm, B)
        norm += 1
        retention()
        retention_out()
        latent()
        ph_ro = PH["ret_out"]
        dve.wait_ge(gate_on, 2)

        def ret_step(i, j, k):
            m = j + 4 * i
            dve.wait_ge(panel_used, ph_ro.p0 + j + 1 + 4 * i)
            V.tensor_tensor(mg["r"][:, m, :], bank[(ph_ro.b0 + j) % 4][:, B], ml["g"][:, m, :],
                            ALU.mult).then_inc(bank_free, 1)
            split_lo(ph_ro, 0, i, j, k)
        dve_steps(ph_ro, 0, 8, ret_step)
        ph_mo = PH["mla_out"]
        for j in range(4):
            dve.wait_ge(panel_used, ph_mo.p0 + j + 1)
            for u in range(2):
                m = 2 * j + u
                V.tensor_tensor(up[:, u, :], bank[(ph_mo.b0 + m) % 4][:, B], ml["g"][:, 8 + m, :],
                                ALU.mult).then_inc(bank_free, 1)
                dve.wait_ge(bank_free, ph_mo.t0 + m + 5)
                V.tensor_tensor(hid[:, u, :], up[:, u, :], mg["r"][:, m, :], ALU.add).then_inc(y_ready, 1)
            split_lo(ph_mo, 0, 0, j, K8)
            for u in range(2):
                m = 2 * j + u
                dve.wait_ge(y_hi, YBASE["mrg"] + m + 1)
                V.tensor_tensor(mg["yl2"][:, m, :], hid[:, u, :], mg["yh2"][:, m, :].bitcast(F32),
                                ALU.subtract).then_inc(y_lo, 1)
        residual(PH["w_o"], ("ffn_w2", 0), B, norm, B)
        norm_inv(norm, B)
        norm += 1
        feed_forward(PH["up4"], DEPTH, B)
        residual(PH["down4"], None, B, norm, B)
        norm_inv(norm, B)
        for m in range(C):
            V.scalar_tensor_tensor(out=x[:, m, A], in0=x[:, m, A], scalar=v("final_w", m), in1=rinv[:, A],
                                   op0=ALU.mult, op1=ALU.mult).then_inc(out_ready, 1)

    ctx.close()


def shape_constants():
    f = np.float32
    con = np.zeros((P, NCON), f)
    con[:, CON["ident"]:CON["ident"] + P] = np.eye(P)
    con[:, CON["ones"]:CON["ones"] + P] = 1
    i = np.arange(P)
    con[:, CON["pair_ones"]:CON["pair_ones"] + P] = i[:, None] // HD == i[None] // HD
    qc, kc = i % GW, np.arange(GW)
    c0 = np.clip(qc - 8, 0, GW - 16)[:, None]
    con[:, CON["colmask"]:CON["colmask"] + GW] = np.where((kc >= c0) & (kc < c0 + 16), 0, -1e30)

    def rope(rows, half, first):
        inv = (f(10000.0) ** (-np.arange(half, dtype=f) / f(half))).astype(f)
        ang = (np.arange(L, dtype=f)[:, None] * inv[None]).astype(f)
        cos, sin, rot = np.ones((P, L), f), np.zeros((P, L), f), np.zeros((P, P), f)
        for r in range(first, rows):
            d = (r - first) % (2 * half)
            cos[r], sin[r] = np.cos(ang[:, d % half]), np.sin(ang[:, d % half])
            if d < half:
                rot[r + half, r] = -1
            else:
                rot[r - half, r] = 1
        return rot, cos, sin

    ret = np.zeros((P, NRTAB), f)
    ret[:, 0:P] = np.eye(P) - 1.0 / P
    rot, cos, sin = rope(P, RDK // 2, 0)
    ret[:, RTAB["rot"]:RTAB["rot"] + P] = rot
    ret[:, RTAB["cos"]:RTAB["cos"] + L] = cos
    ret[:, RTAB["sin"]:RTAB["sin"] + L] = sin
    for r in range(3):
        j, q = r * P + i[:, None], np.arange(L)[None]
        ret[:, RTAB["back"] + r * L:RTAB["back"] + (r + 1) * L] = np.maximum(q - j, 0)
        ret[:, RTAB["ahead"] + r * L:RTAB["ahead"] + (r + 1) * L] = np.maximum(j - q, 0)
    mla = np.zeros((P, NMTAB), f)
    rot, cos, sin = rope(MQK, ROPE // 2, NOPE)
    mla[:, 0:P], mla[:, P:P + L], mla[:, P + L:] = rot, cos, sin

    t = np.arange(SEQ, dtype=np.float64)
    w = 2 * np.pi * np.outer(t, t) / NFFT
    alt = np.where(np.arange(SEQ) % 2, -1.0, 1.0)
    fcos, fsin = np.cos(w), np.sin(w)
    fsin[:, 0] = alt
    last = fcos[:, 0:P].copy()
    last[:, 0] = alt
    fdft = np.concatenate([fcos, fsin, last], 1).astype(f).reshape(2, P, -1).transpose(1, 0, 2)
    icos, isin = 2 * np.cos(w) / NFFT, 2 * np.sin(w) / NFFT
    icos[0] = 1 / NFFT
    isin[0] = alt / NFFT
    idft = np.concatenate([icos, isin], 0).astype(f).reshape(4, P, SEQ).transpose(1, 0, 2)

    tt = np.linspace(0.0, 1.0, SEQ, dtype=f)
    bands = np.linspace(1e-4, 15, 16, dtype=f)
    ang = (f(2.0 * math.pi) * np.arange(SEQ, dtype=f)[:, None] / f(SEQ) * bands).astype(f)
    z = np.concatenate([tt[:, None], np.cos(ang), -np.sin(ang)], -1).astype(f)
    lt = math.log(1e-2)
    deltas = np.abs(np.linspace(lt / 1.5, lt / 0.3, D, dtype=f))
    decay = np.exp(-tt[:, None] * deltas).astype(f).reshape(2, P, D).transpose(1, 0, 2)
    return con, ret, mla, fdft, idft, z.T, decay


def lay_out(w):
    cols = lambda t: t.reshape(-1, P).T

    def tiles(m, starts=None):
        k = m.shape[0] // P
        if starts is None:
            starts = range(0, m.shape[1], P)
        r = m.reshape(k, P, m.shape[1])
        return [np.ascontiguousarray(r[:, :, s:s + P].transpose(1, 0, 2)) for s in starts]

    w8, w11 = [], []

    def add(ts):
        w8.extend(t.reshape(P, -1) for t in ts)

    def add_ffn(g, u, down):
        for p, q in zip(tiles(g), tiles(u)):
            add([p, q])
        for t in tiles(down):
            w11.extend([t[:, :K11].reshape(P, -1), t[:, K11:].reshape(P, -1)])

    mix_in = [w["a_w_in"][0], w["b_w_qkv"][0], w["c_w_in"][0], w["a_w_in"][1]]
    mix_out = [w["a_w_out"][0], w["b_w_out"][0], w["c_w_out"][0], w["a_w_out"][1]]
    for layer in range(DEPTH):
        ts = tiles(mix_in[layer])
        if KINDS[layer] == "conv":
            ts = ts[8:24] + ts[0:8]
        add(ts)
        add(tiles(mix_out[layer]))
        add_ffn(w["f_w13"][layer][:, :FF], w["f_w13"][layer][:, FF:], w["f_w2"][layer])
    wi = w["w_in_2"][0]
    add(tiles(wi, range(0, 3072, P)))
    add(tiles(wi, [3072, 3200, 3328, 3456, 3584, 3712 - NOPE]))
    add(tiles(wi, range(3744, 5792, P)))
    add(tiles(w["w_ret_out_2"][0]))
    mo = tiles(w["w_mla_out_2"][0])
    add([np.concatenate([mo[2 * i], mo[2 * i + 1]], 1) for i in range(4)])
    add(tiles(w["w_o_2"][0]))
    add_ffn(w["w_ffn_gate_2"][0], w["w_ffn_up_2"][0], w["w_ffn_down_2"][0])

    pad = lambda t: np.concatenate([t, np.zeros(P - t.shape[0], t.dtype)])[:, None]
    vec = np.concatenate([
        cols(w["norm_mix_g"]), cols(w["norm_ffn_g"]), cols(w["a_conv_w"]), cols(w["c_short_w"]),
        cols(w["c_short_b"]), cols(w["c_f_skip"]), cols(w["norm_mix_w_2"]), cols(w["norm_ffn_w_2"]),
        cols(w["norm_final_w_2"]), cols(w["ret_gn_w_2"]), cols(w["mla_q_norm_w_2"]), cols(w["mla_kv_norm_w_2"]),
        np.tile(w["b_q_norm_g"][0], 2)[:, None], np.tile(w["b_k_norm_g"][0], 2)[:, None],
        pad(w["c_f_b1"][0]), pad(w["c_f_b2"][0]), pad(w["c_f_freq"][0])], 1)
    con, ret_tab, mla_tab, fdft, idft, zT, decay = shape_constants()
    u, c = np.arange(P)[:, None, None] // GW, np.arange(P)[:, None, None] % GW
    j, k = np.arange(6)[None, :, None], np.arange(GW)[None, None, :]
    bias = w["b_rpb"][0][:, 5 - u + j, np.clip(k - c + 15, 0, 30)].transpose(1, 0, 2, 3)
    chunked = lambda t: t.reshape(-1, P, t.shape[-1]).transpose(1, 0, 2)
    return {
        "xT": chunked(w["x"][0].T), "metaT": chunked(w["meta_tokens_2"].T), "vec": vec, "con": con,
        "w8": np.stack(w8), "w11": np.stack(w11), "bias": bias,
        "filt_in": np.concatenate([zT, w["c_f_w1"][0]], 1), "filt_w2": w["c_f_w2"][0],
        "filt_w3": w["c_f_w3"][0].reshape(FHID, 4, D), "fdft": fdft, "idft": idft, "decay": decay,
        "ret_tab": ret_tab, "mla_tab": mla_tab,
        "decays": np.stack([w["ret_decay_fwd_2"][0], w["ret_decay_bwd_2"][0]])[None],
        "uq": chunked(w["w_uq_2"][0]), "uk": chunked(w["w_uk_2"][0]), "uv": chunked(w["w_uv_2"][0]),
    }


def kernel(**inputs):
    import concourse.bacc as bacc
    from concourse.bass_utils import run_bass_kernel_spmd

    arrays = {n: np.ascontiguousarray(t) for n, t in lay_out({k: np.asarray(t) for k, t in inputs.items()}).items()}
    nc = bacc.Bacc("TRN2", target_bir_lowering=False, num_devices=1)
    args = {n: nc.dram_tensor(f"in_{n}", t.shape, mybir.dt.from_np(t.dtype), kind="ExternalInput").ap()
            for n, t in arrays.items()}
    out = nc.dram_tensor("out", (P, C, SEQ), F32, kind="ExternalOutput").ap()
    build(nc, args, out)
    got = run_bass_kernel_spmd(nc, [{f"in_{n}": t for n, t in arrays.items()}], core_ids=[0]).results[0]["out"]
    return np.ascontiguousarray(got.transpose(2, 1, 0).reshape(1, SEQ, D))
```
